# Optimizing a Trainium2 kernel written in Bass

```python
import jax
import jax.numpy as jnp
from jax import lax
import numpy as np

D_MODEL = 2048
BATCH = 1
SEQ = 256
DEPTH = 1

CHUNK = 64
PLE_DIM = 256
D_FF = 5632
GDN_HEADS = 8
GDN_DK = 128
GDN_DV = 128
GDN_QKV = 2 * GDN_HEADS * GDN_DK + GDN_HEADS * GDN_DV
GDN_W = GDN_HEADS * GDN_DV
CONV_K = 4
ATT_HEADS = 8
ATT_DH = 128
ATT_W = ATT_HEADS * ATT_DH
LEFT_CHUNKS = 8
BAND = (LEFT_CHUNKS + 1) * CHUNK
MAX_REL = 128
N_REL = (CHUNK - 1) + MAX_REL + 1
EPS = 1e-6
NEG_INF = -1e30
IN_SPLITS = (GDN_QKV, GDN_W, GDN_HEADS, GDN_HEADS, 3 * ATT_W, D_MODEL, D_MODEL)
IN_COLS = sum(IN_SPLITS)

kernel_name = "hybrid_gdn_bandattn_macaron_block"

def rmsnorm(x, w, eps=EPS):
    xf = x.astype(jnp.float32)
    y = xf * lax.rsqrt(jnp.mean(xf * xf, axis=-1, keepdims=True) + eps)
    return (y * w.astype(jnp.float32)).astype(x.dtype)

def l2norm(x, eps=EPS):
    xf = x.astype(jnp.float32)
    return xf * lax.rsqrt(jnp.sum(xf * xf, axis=-1, keepdims=True) + eps)

def swiglu_ffn(h, w_gu, w_down):
    g, u = jnp.split(h @ w_gu, 2, axis=-1)
    return (jax.nn.silu(g) * u) @ w_down

def causal_short_conv(x, w):
    ksz = w.shape[0]
    seqlen = x.shape[1]
    xp = jnp.pad(x, ((0, 0), (ksz - 1, 0), (0, 0)))
    y = xp[:, 0:seqlen] * w[0]
    for j in range(1, ksz):
        y = y + xp[:, j:j + seqlen] * w[j]
    return y

def to_chunks(t):
    b, s, h, d = t.shape
    return t.reshape(b, s // CHUNK, CHUNK, h, d).transpose(0, 3, 1, 2, 4)

def to_chunks_h(t):
    b, s, h = t.shape
    return t.reshape(b, s // CHUNK, CHUNK, h).transpose(0, 3, 1, 2)

def gated_delta_rule_chunked(q, k, v, g, beta):
    c = q.shape[-2]
    dv = v.shape[-1]
    gc = jnp.cumsum(g, axis=-1)
    idx = jnp.arange(c)
    incl = idx[:, None] >= idx[None, :]
    strict = idx[:, None] > idx[None, :]
    diff = gc[..., :, None] - gc[..., None, :]
    decay = jnp.where(incl, jnp.exp(jnp.where(incl, diff, 0.0)), 0.0)
    kb = k * beta[..., None]
    lmat = jnp.where(strict, jnp.einsum('bhnid,bhnjd->bhnij', kb, k) * decay, 0.0)
    rhs = jnp.concatenate([v * beta[..., None], kb * jnp.exp(gc)[..., None]], axis=-1)
    sol = lax.linalg.triangular_solve(lmat + jnp.eye(c, dtype=lmat.dtype), rhs,
                                      left_side=True, lower=True, unit_diagonal=True)
    u, w = sol[..., :dv], sol[..., dv:]
    aqk = jnp.einsum('bhnid,bhnjd->bhnij', q, k) * decay
    q_dec = q * jnp.exp(gc)[..., None]
    k_tail = k * jnp.exp(gc[..., -1:] - gc)[..., None]
    tail = jnp.exp(gc[..., -1])

    def step(state, xs):
        u_c, w_c, aqk_c, qd_c, kt_c, tl_c = xs
        v_new = u_c - jnp.einsum('bhcd,bhde->bhce', w_c, state)
        o_c = (jnp.einsum('bhcd,bhde->bhce', qd_c, state)
               + jnp.einsum('bhcj,bhje->bhce', aqk_c, v_new))
        state = state * tl_c[..., None, None] + jnp.einsum('bhcd,bhce->bhde', kt_c, v_new)
        return state, o_c

    xs = tuple(jnp.moveaxis(t, 2, 0) for t in (u, w, aqk, q_dec, k_tail, tail))
    s0 = jnp.zeros(q.shape[:2] + (q.shape[-1], dv), jnp.float32)
    _, o = lax.scan(step, s0, xs)
    return jnp.moveaxis(o, 0, 2)

def gated_deltanet_branch(qkv, z, a_raw, b_raw, conv_w, a_log, dt_bias, norm_w):
    bsz, seqlen, _ = qkv.shape
    qkv = jax.nn.silu(causal_short_conv(qkv, conv_w))
    q, k, v = jnp.split(qkv, [GDN_HEADS * GDN_DK, 2 * GDN_HEADS * GDN_DK], axis=-1)
    q = l2norm(q.reshape(bsz, seqlen, GDN_HEADS, GDN_DK)) * (GDN_DK ** -0.5)
    k = l2norm(k.reshape(bsz, seqlen, GDN_HEADS, GDN_DK))
    v = v.reshape(bsz, seqlen, GDN_HEADS, GDN_DV).astype(jnp.float32)
    g = -jnp.exp(a_log.astype(jnp.float32)) * jax.nn.softplus(
        a_raw.astype(jnp.float32) + dt_bias.astype(jnp.float32))
    beta = jax.nn.sigmoid(b_raw.astype(jnp.float32))
    o = gated_delta_rule_chunked(to_chunks(q), to_chunks(k), to_chunks(v),
                                 to_chunks_h(g), to_chunks_h(beta))
    o = o.transpose(0, 2, 3, 1, 4).reshape(bsz, seqlen, GDN_HEADS, GDN_DV)
    zf = z.reshape(bsz, seqlen, GDN_HEADS, GDN_DV).astype(jnp.float32)
    o = rmsnorm(o, norm_w) * jax.nn.silu(zf)
    return o.reshape(bsz, seqlen, GDN_W).astype(z.dtype)

def gather_band(t):
    nc = t.shape[1]
    tp = jnp.pad(t, ((0, 0), (LEFT_CHUNKS, 0), (0, 0), (0, 0), (0, 0)))
    return jnp.concatenate([tp[:, j:j + nc] for j in range(LEFT_CHUNKS + 1)], axis=2)

def band_attention_branch(qkv, q_norm_w, k_norm_w, rel_bias):
    bsz, seqlen, _ = qkv.shape
    nc = seqlen // CHUNK
    q, k, v = jnp.split(qkv, 3, axis=-1)
    shp = (bsz, nc, CHUNK, ATT_HEADS, ATT_DH)
    q = rmsnorm(q.reshape(shp), q_norm_w)
    k_band = gather_band(rmsnorm(k.reshape(shp), k_norm_w))
    v_band = gather_band(v.reshape(shp))
    qpos = np.arange(CHUNK)[:, None]
    kpos = np.arange(BAND)[None, :] - LEFT_CHUNKS * CHUNK
    rel_idx = np.clip(qpos - kpos, -(CHUNK - 1), MAX_REL) + (CHUNK - 1)
    bias = rel_bias[:, rel_idx].astype(jnp.float32)
    valid = jnp.asarray((np.arange(nc)[:, None] - LEFT_CHUNKS
                         + np.arange(BAND)[None, :] // CHUNK) >= 0)
    s = jnp.einsum('bnqhd,bnkhd->bhnqk', q, k_band).astype(jnp.float32) * (ATT_DH ** -0.5)
    s = jnp.where(valid[:, None, :], s + bias[:, None], NEG_INF)
    pr = jax.nn.softmax(s, axis=-1).astype(v_band.dtype)
    o = jnp.einsum('bhnqk,bnkhd->bnqhd', pr, v_band)
    return o.reshape(bsz, seqlen, ATT_W)

def setup_inputs(seed: int = 0) -> dict:
    key = jax.random.key(seed)
    ks = jax.random.split(key, 24)
    f32 = jnp.float32

    def dense(k, shape):
        return jax.random.normal(k, shape, f32) * (shape[-2] ** -0.5)

    def gain(k, n):
        return 1.0 + 0.05 * jax.random.normal(k, (DEPTH, n), f32)

    dt = jnp.exp(jax.random.uniform(ks[9], (DEPTH, GDN_HEADS), f32,
                                    float(np.log(1e-3)), float(np.log(1e-1))))
    dt_bias = dt + jnp.log(-jnp.expm1(-dt))
    return {
        'x': jax.random.normal(ks[0], (BATCH, SEQ, D_MODEL), f32),
        'p': jax.random.normal(ks[1], (DEPTH, BATCH, SEQ, PLE_DIM), f32),
        'ffn1_norm': gain(ks[2], D_MODEL),
        'ffn1_w_gu': dense(ks[3], (DEPTH, D_MODEL, 2 * D_FF)),
        'ffn1_w_down': dense(ks[4], (DEPTH, D_FF, D_MODEL)),
        'mix_norm': gain(ks[5], D_MODEL),
        'w_in': dense(ks[6], (DEPTH, D_MODEL, IN_COLS)),
        'conv_w': 0.5 * jax.random.normal(ks[7], (DEPTH, CONV_K, GDN_QKV), f32),
        'a_log': jnp.log(jax.random.uniform(ks[8], (DEPTH, GDN_HEADS), f32, 1.0, 16.0)),
        'dt_bias': dt_bias,
        'gdn_norm': gain(ks[10], GDN_DV),
        'q_norm': gain(ks[11], ATT_DH),
        'k_norm': gain(ks[12], ATT_DH),
        'rel_bias': 0.5 * jax.random.normal(ks[13], (DEPTH, ATT_HEADS, N_REL), f32),
        'w_branch_a': dense(ks[14], (DEPTH, GDN_W, D_MODEL)),
        'w_branch_b': dense(ks[15], (DEPTH, ATT_W, D_MODEL)),
        'w_out': dense(ks[16], (DEPTH, D_MODEL, D_MODEL)),
        'ffn2_norm': gain(ks[17], D_MODEL),
        'ffn2_w_gu': dense(ks[18], (DEPTH, D_MODEL, 2 * D_FF)),
        'ffn2_w_down': dense(ks[19], (DEPTH, D_FF, D_MODEL)),
        'ple_norm': gain(ks[20], D_MODEL),
        'ple_gate': dense(ks[21], (DEPTH, D_MODEL, D_MODEL)),
        'ple_proj': dense(ks[22], (DEPTH, PLE_DIM, D_MODEL)),
    }

def reference(x, p, ffn1_norm, ffn1_w_gu, ffn1_w_down, mix_norm, w_in, conv_w, a_log,
              dt_bias, gdn_norm, q_norm, k_norm, rel_bias, w_branch_a, w_branch_b, w_out,
              ffn2_norm, ffn2_w_gu, ffn2_w_down, ple_norm, ple_gate, ple_proj):
    split_at = [int(s) for s in np.cumsum(IN_SPLITS)[:-1]]
    for i in range(DEPTH):
        x = x + 0.5 * swiglu_ffn(rmsnorm(x, ffn1_norm[i]), ffn1_w_gu[i], ffn1_w_down[i])
        h = rmsnorm(x, mix_norm[i])
        qkv_a, z_a, a_raw, b_raw, qkv_b, gate_a, gate_b = jnp.split(h @ w_in[i], split_at, axis=-1)
        ya = gated_deltanet_branch(qkv_a, z_a, a_raw, b_raw, conv_w[i], a_log[i],
                                   dt_bias[i], gdn_norm[i])
        yb = band_attention_branch(qkv_b, q_norm[i], k_norm[i], rel_bias[i])
        mixed = (jax.nn.sigmoid(gate_a) * (ya @ w_branch_a[i])
                 + jax.nn.sigmoid(gate_b) * (yb @ w_branch_b[i]))
        x = x + mixed @ w_out[i]
        x = x + 0.5 * swiglu_ffn(rmsnorm(x, ffn2_norm[i]), ffn2_w_gu[i], ffn2_w_down[i])
        x = x + jax.nn.sigmoid(rmsnorm(x, ple_norm[i]) @ ple_gate[i]) * (p[i] @ ple_proj[i])
    return x


_drawn_inputs = setup_inputs


def setup_inputs(seed=0):
    import zlib

    import numpy as np

    out = dict(_drawn_inputs(seed))
    spreads = {}
    factors = {'gdn_norm': 3.629, 'q_norm': 8.0, 'k_norm': 8.0, 'ffn2_norm': 3.247, 'ple_norm': 146.831}
    for name, (base, spread) in spreads.items():
        noise = np.random.default_rng([zlib.crc32(name.encode()), seed]).standard_normal(out[name].shape)
        drawn = base * np.exp(spread * noise) if base else spread * noise
        out[name] = jnp.asarray(drawn.astype(out[name].dtype))
    for name, factor in factors.items():
        out[name] = (out[name] * factor).astype(out[name].dtype)
    return out
```

```python
from contextlib import ExitStack

import numpy as np

import concourse.bass as bass
from concourse import mybir

F32 = mybir.dt.float32
F32R = mybir.dt.float32r
ACT = mybir.ActivationFunctionType
ALU = mybir.AluOpType
AX = mybir.AxisListType

P = 128
T = 256
D = 2048
FF = 5632
PLE = 256
HEADS = 8
DH = 128
CONV_K = 4
CHUNK = 64
GC = 128
MAX_REL = 128
EPS = 1e-6
NEG_INF = -1e30

KT = D // P
FT = FF // P
UK = 4
UC = UK * P
RAW = 8
HL = 4
CHUNK_SLOTS = RAW // 2
LEVELS = 7

HEAD_TILES = 7
HEAD_UNITS = HEAD_TILES * KT // UK
GHOST_GATES = 8
GATES = 2 * KT

U_GU1 = 0
U_DOWN1 = U_GU1 + FT * 2 * KT // UK
U_HEADS = U_DOWN1 + KT * FT // UK
U_GHOST = U_HEADS + HEADS * HEAD_UNITS
U_GATES = U_GHOST + GHOST_GATES * KT // UK
U_BRANCH = U_GATES + (GATES - GHOST_GATES) * KT // UK
U_OUT = U_BRANCH + KT * 2 * HEADS // UK
U_GU2 = U_OUT + KT * KT // UK
U_DOWN2 = U_GU2 + FT * 2 * KT // UK
U_PROJ = U_DOWN2 + KT * FT // UK
U_PLE = U_PROJ + KT * (PLE // P) // UK
UNITS = U_PLE + KT * KT // UK

T_GU1 = 0
T_DOWN1 = T_GU1 + FT
T_HEADS = T_DOWN1 + KT
T_GHOST = T_HEADS + HEADS * HEAD_TILES
T_BRANCH = T_GHOST + GATES
T_OUT = T_BRANCH + KT
T_GU2 = T_OUT + KT
T_DOWN2 = T_GU2 + FT
T_PROJ = T_DOWN2 + KT
T_PLE = T_PROJ + KT // 2

C_IDENT, C_ONES, C_UPPER, C_MASKS = 0, 1, 2, 3
N_CONST = C_MASKS + LEVELS
P_NORMS = 0
P_CONV = P_NORMS + 4 * KT
P_GDN_NORM = P_CONV + HEADS * 3 * CONV_K
P_Q_NORM = P_GDN_NORM + 1
P_K_NORM = P_Q_NORM + 1
P_DT = P_K_NORM + 1
P_ALOG = P_DT + HEADS
N_PARAM = P_ALOG + HEADS
BANK_OF_HEAD_TILE = [0, 1, 2, 3, 0, 1, 2]
K_G, K_GC, K_BETA, K_NEG_BETA, K_EXP_GC, K_TAIL, N_COL = 0, 2, 4, 6, 7, 8, 9
SCORES = GC + T


def build(nc, wstream, x_in, p_in, consts_in, params_in, wab_in, bias_in, y_out):
    ctx = ExitStack()
    with ctx:
        def sb(name, shape, dt=F32, stack=ctx):
            return stack.enter_context(nc.sbuf_tensor(name, shape, dt))

        def sem(name):
            return ctx.enter_context(nc.semaphore(name))

        raw = sb("raw", [P, RAW, UC])
        w_hi = sb("w_hi", [P, HL, UC], F32R)
        w_lo = sb("w_lo", [P, HL, UC], F32R)
        x = sb("x", [P, KT, T])
        xw = sb("xw", [P, KT, 2 * T], F32R)
        const = sb("const", [P, N_CONST, P])
        par = sb("par", [P, N_PARAM])
        eps = sb("eps", [P, 1])
        unread = sb("unread", [P, 1])
        r = sb("r", [P, T])
        r_ln = sb("r_ln", [P, T])
        xsq = sb("xsq", [P, 2, T])
        acc = sb("acc", [P, T])
        part = sb("part", [P, 2, 2 * T])
        whole = sb("whole", [P, 2, 2 * T])
        act2 = sb("act2", [P, 2, T])
        prod = sb("prod", [P, 2, T])

        ffn = ExitStack()
        hid = sb("hid", [P, FT, 2 * T], F32R, ffn)
        ffn.close()
        mix = ExitStack()
        ya = sb("ya", [P, HEADS, 2 * T], F32R, mix)
        yb = sb("yb", [P, HEADS, 2 * T], F32R, mix)
        gdn = ExitStack()
        sb("first_gates", [P, GHOST_GATES, T], F32, gdn)
        wab = sb("wab", [P, KT * 2 * HEADS], F32, gdn)
        wab_hi = sb("wab_hi", [P, KT * 2 * HEADS], F32R, gdn)
        wab_lo = sb("wab_lo", [P, KT * 2 * HEADS], F32R, gdn)
        bias = sb("bias", [P, HEADS, SCORES], F32, gdn)

        def gs(name, shape):
            return sb(name, shape, F32, gdn)

        padded = gs("padded", [P, 3, CONV_K - 1 + T])
        taps = gs("taps", [P, 3 * CONV_K])
        tap = gs("tap", [P, T])
        conv = gs("conv", [P, 4, T])
        qkvz = gs("qkvz", [P, 2, 4, T])
        qk_sq = gs("qk_sq", [P, 2, T])
        qn = gs("qn", [P, T])
        kn = gs("kn", [P, T])
        qe = gs("qe", [P, GC])
        ab = gs("ab", [P, 2, 2 * HEADS])
        r_tok = gs("r_tok", [P, 2])
        t16 = gs("t16", [P, 8, 2 * HEADS])
        cols = gs("cols", [P, N_COL, HEADS])
        hcol = gs("hcol", [P, 2, N_COL])
        upper_g = gs("upper_g", [P, 2, GC])
        v_tok = gs("v_tok", [P, 2, DH])
        k_tail = gs("k_tail", [P, DH])
        decay = gs("decay", [P, 4, GC])
        exp_gc = gs("exp_gc", [P, GC])
        a_qk = gs("a_qk", [P, 2, GC])
        lmat = gs("lmat", [P, 2, GC])
        cmat = gs("cmat", [P, LEVELS, 2, GC])
        inv = gs("inv", [P, 4, GC])
        t1 = gs("t1", [P, 2, GC])
        rhs0 = gs("rhs0", [P, DH])
        rhs1 = gs("rhs1", [P, 2, DH])
        v_new = gs("v_new", [P, 2, DH])
        state = gs("state", [P, DH])
        o_gdn = gs("o_gdn", [P, T])
        o_sq = gs("o_sq", [P, T])
        y_gdn = gs("y_gdn", [P, 2, T])
        att = gs("att", [P, 3, T])
        att_sq = gs("att_sq", [P, 2, T])
        att_n = gs("att_n", [P, 2, T])
        av_tok = gs("av_tok", [P, 2, DH])
        score = gs("score", [P, SCORES])
        prob_t = gs("prob_t", [P, SCORES])
        smax = gs("smax", [P, 2])
        sneg = gs("sneg", [P, 2])
        ssum = gs("ssum", [P, 2])
        sinv = gs("sinv", [P, 2])
        gdn.close()
        gates = sb("gates", [P, GATES, T], F32, mix)
        mixed = sb("mixed", [P, KT, 2 * T], F32R, mix)
        sig = sb("sig", [P, 2, 2, T], F32, mix)
        mixed_f = sb("mixed_f", [P, 2, T], F32, mix)
        mix.close()
        ple = ExitStack()
        p_raw = sb("p_raw", [P, PLE // P, T], F32, ple)
        p_hl = sb("p_hl", [P, PLE // P, 2 * T], F32R, ple)
        emb = sb("emb", [P, KT, T], F32, ple)
        gate_s = sb("gate_s", [P, 2, T], F32, ple)
        y = sb("y", [P, KT, T], F32, ple)
        ple.close()

        ps = ctx.enter_context(nc.psum_tensor("ps", [P, 8, 2 * T], F32))
        ident, ones, upper = const[:, C_IDENT, :], const[:, C_ONES, :], const[:, C_UPPER, :]

        def both(ap):
            return ap.unsqueeze(1).to_broadcast([P, 2, ap.shape[-1]])

        chunk_landed = [sem(f"chunk_landed{i}") for i in range(CHUNK_SLOTS)]
        x_landed = [sem(f"x_landed{i}") for i in range(4)]
        const_landed = sem("const_landed")
        par_landed = sem("par_landed")
        mix_landed = sem("mix_landed")
        p_landed = sem("p_landed")
        y_stored = sem("y_stored")
        hi_ready = sem("hi_ready")
        lo_ready = sem("lo_ready")
        unit_used = sem("unit_used")
        part_ready = sem("part_ready")
        tile_free = sem("tile_free")
        x_new = sem("x_new")
        xsq_ready = sem("xsq_ready")
        acc_added = sem("acc_added")
        xw_hi = sem("xw_hi")
        xw_lo = sem("xw_lo")
        norm_summed = sem("norm_summed")
        r_logged = sem("r_logged")
        r_ready = sem("r_ready")
        eps_set = sem("eps_set")
        gu_scaled = sem("gu_scaled")
        gu_silu = sem("gu_silu")
        hid_new = sem("hid_new")
        hid_hi = sem("hid_hi")
        hid_lo = sem("hid_lo")
        scaled = sem("scaled")
        pad_zero = sem("pad_zero")
        conv_steps = sem("conv_steps")
        taps_ready = sem("taps_ready")
        silu_done = sem("silu_done")
        qk_sq_ready = sem("qk_sq_ready")
        qk_summed = sem("qk_summed")
        v_turned = sem("v_turned")
        v_copied = sem("v_copied")
        qk_steps = sem("qk_steps")
        qk_normed = sem("qk_normed")
        wab_split = sem("wab_split")
        wab_lo_ready = sem("wab_lo_ready")
        ab_ready = sem("ab_ready")
        ab_steps = sem("ab_steps")
        ab_acts = sem("ab_acts")
        gc_summed = sem("gc_summed")
        hcol_ready = sem("hcol_ready")
        upper_ready = sem("upper_ready")
        gram_ready = sem("gram_ready")
        gc_ready = sem("gc_ready")
        arg_ready = sem("arg_ready")
        decay_ready = sem("decay_ready")
        exp_gc_ready = sem("exp_gc_ready")
        k_tail_ready = sem("k_tail_ready")
        lmat_ready = sem("lmat_ready")
        incl_ready = sem("incl_ready")
        cmat_ready = sem("cmat_ready")
        a_qk_ready = sem("a_qk_ready")
        qe_ready = sem("qe_ready")
        c0_turned = sem("c0_turned")
        inv_ready = sem("inv_ready")
        t1_ready = sem("t1_ready")
        t1_copied = sem("t1_copied")
        step_ready = sem("step_ready")
        rhs0_ready = sem("rhs0_ready")
        v0_ready = sem("v0_ready")
        v0_copied = sem("v0_copied")
        state_ready = sem("state_ready")
        state_copied = sem("state_copied")
        ks_ready = sem("ks_ready")
        rhs1_steps = sem("rhs1_steps")
        v1_ready = sem("v1_ready")
        v1_copied = sem("v1_copied")
        o_ready = sem("o_ready")
        o_copied = sem("o_copied")
        o_sq_ready = sem("o_sq_ready")
        o_summed = sem("o_summed")
        o_steps = sem("o_steps")
        y_steps = sem("y_steps")
        ya_hi = sem("ya_hi")
        ya_lo = sem("ya_lo")
        att_sq_ready = sem("att_sq_ready")
        av_turned = sem("av_turned")
        av_copied = sem("av_copied")
        att_summed = sem("att_summed")
        att_steps = sem("att_steps")
        att_normed = sem("att_normed")
        score_ready = sem("score_ready")
        score_steps = sem("score_steps")
        exp_done = sem("exp_done")
        sinv_ready = sem("sinv_ready")
        prob_ready = sem("prob_ready")
        prob_turned = sem("prob_turned")
        prob_copied = sem("prob_copied")
        att_o_ready = sem("att_o_ready")
        yb_hi = sem("yb_hi")
        yb_lo = sem("yb_lo")
        sig_ready = sem("sig_ready")
        branch_steps = sem("branch_steps")
        mixed_hi = sem("mixed_hi")
        mixed_lo = sem("mixed_lo")
        p_hi = sem("p_hi")
        p_lo = sem("p_lo")
        ple_scaled = sem("ple_scaled")
        ple_sig = sem("ple_sig")
        y_parts = sem("y_parts")

        block = ctx.enter_context(nc.Block())

        @block.sync
        def _(sp):
            sp.dma_start(par[:], params_in).then_inc(par_landed, 16)
            for i in range(4):
                sp.dma_start(x[:, 4 * i:4 * i + 4, :], x_in[:, 4 * i:4 * i + 4, :]).then_inc(x_landed[i], 16)
                sp.dma_start(raw[:, 2 * i:2 * i + 2, :].rearrange("p a b -> p (a b)"),
                             wstream[i]).then_inc(chunk_landed[i], 16)
            sp.dma_start(const[:], consts_in).then_inc(const_landed, 16)

            def load_chunks(i):
                for s in range(CHUNK_SLOTS):
                    sp.wait_ge(lo_ready, i * RAW + 2 * s + 2 - RAW)
                    sp.dma_start(raw[:, 2 * s:2 * s + 2, :].rearrange("p a b -> p (a b)"),
                                 wstream[CHUNK_SLOTS * i + s]).then_inc(chunk_landed[s], 16)

            with sp.Fori(1, U_HEADS // RAW + 1) as i:
                load_chunks(i)
            sp.wait_ge(unit_used, U_HEADS)
            sp.dma_start(wab[:], wab_in).then_inc(mix_landed, 16)
            sp.dma_start(bias[:], bias_in).then_inc(mix_landed, 16)
            with sp.Fori(U_HEADS // RAW + 1, U_PROJ // RAW) as i:
                load_chunks(i)
            load_chunks(U_PROJ // RAW)
            sp.wait_ge(unit_used, U_PROJ)
            sp.dma_start(p_raw[:], p_in).then_inc(p_landed, 16)
            with sp.Fori(U_PROJ // RAW + 1, UNITS // RAW) as i:
                load_chunks(i)

        @block.scalar
        def _(act):
            def split_hi(ub, k):
                if k % 2 == 0:
                    act.wait_ge(chunk_landed[(k // 2) % CHUNK_SLOTS], ub * 2 + (16 * (k // RAW) + 16))
                if not (isinstance(ub, int) and ub + k < HL):
                    act.wait_ge(unit_used, ub + (k + 1 - HL))
                nc.scalar.activation(w_hi[:, k % HL, :], raw[:, k % RAW, :], ACT.Copy).then_inc(hi_ready, 1)

            def copy_part(tile, par_, used, bank, pair=False):
                act.wait_ge(unit_used, used)
                if not (isinstance(tile, int) and tile < 2):
                    act.wait_ge(tile_free, tile - 1)
                if pair:
                    nc.scalar.activation(part[:, par_, :].rearrange("p (a b) -> p a b", a=2),
                                         ps[:, bank:bank + 2, T:], ACT.Copy).then_inc(part_ready, 1)
                else:
                    nc.scalar.activation(part[:, par_, 0:T], ps[:, bank, T:], ACT.Copy).then_inc(part_ready, 1)

            def x_block(round_, m, s):
                if round_ > 0:
                    act.wait_ge(x_new, m + (1 + KT * (round_ - 1)))
                if not (isinstance(m, int) and round_ == 0 and m < 2):
                    act.wait_ge(acc_added, m + (KT * round_ - 1))
                nc.scalar.activation(xsq[:, s, :], x[:, m, :], ACT.Square).then_inc(xsq_ready, 1)
                nc.scalar.activation(xw[:, m, 0:T], x[:, m, :], ACT.Copy,
                                     scale=par[:, bass.ds(m + (P_NORMS + KT * round_), 1)]).then_inc(xw_hi, 1)

            def norm_factor(round_):
                act.wait_ge(norm_summed, round_ + 1)
                nc.scalar.activation(r_ln[:], ps[:, 4, 0:T], ACT.Ln, bias=eps[:], scale=1.0 / D).then_inc(r_logged, 1)
                act.wait_ge(r_logged, round_ + 1)
                nc.scalar.activation(r[:], r_ln[:], ACT.Exp, scale=-0.5).then_inc(r_ready, 1)

            def gu_silu_step(n, p):
                act.wait_ge(gu_scaled, n + 1)
                nc.scalar.activation(act2[:, p, :], whole[:, p, 0:T], ACT.Silu).then_inc(gu_silu, 1)

            def gu_hi_step(n, f, p):
                act.wait_ge(hid_new, n + 1)
                nc.scalar.activation(hid[:, f, 0:T], prod[:, p, :], ACT.Copy).then_inc(hid_hi, 1)

            act.wait_ge(par_landed, 16)
            for m in range(KT):
                if m % 4 == 0:
                    act.wait_ge(x_landed[m // 4], 16)
                x_block(0, m, m % 2)
                if m % 4 == 3:
                    split_hi(0, m // 4)

            def gu_tile(ub, k0, n0, f, p, u0, t0, first, older):
                for j in range(8):
                    if j == 1 and older:
                        gu_hi_step(n0 + f - 2, f - 2, p)
                    if first and k0 + j == 9:
                        norm_factor(first - 1)
                    if j == 4 and (not first or k0 > 0):
                        copy_part(t0 + f - 1, (1 - p), u0 + 8 * f, 2 * (1 - p), pair=True)
                    if j == 7 and (not first or k0 > 0):
                        gu_silu_step(n0 + f - 1, 1 - p)
                    if n0 == FT and first and k0 == 0:
                        out_tail(j)
                    if not (first == 1 and k0 + j < 4):
                        split_hi(ub, k0 + j)

            def out_tail(j):
                m = 14 + j // 4
                if j % 4 == 0:
                    copy_part(T_OUT + m, m % 2, U_OUT + 4 * (m + 1), m % 4)
                if j % 4 == 2:
                    x_block(2, m, m % 2)

            def gu_phase(round_, n0, u0, t0):
                gu_tile(u0, 0, n0, 0, 0, u0, t0, round_ + 1, False)
                gu_tile(u0, 8, n0, 1, 1, u0, t0, round_ + 1, False)
                with act.Fori(1, FT // 2) as i:
                    gu_tile(i * 16 + u0, 0, n0, i * 2, 0, u0, t0, 0, True)
                    gu_tile(i * 16 + u0, 8, n0, i * 2 + 1, 1, u0, t0, 0, True)

            def down_phase(round_, n0, u0, t0, gu_u, gu_t):
                for m in range(KT):
                    for j in range(11):
                        k = 11 * m + j
                        if m == 0:
                            if j == 1:
                                gu_hi_step(n0 + FT - 2, FT - 2, 0)
                            if j == 4:
                                copy_part(gu_t + FT - 1, 1, gu_u + 8 * FT, 2, pair=True)
                            if j == 7:
                                gu_silu_step(n0 + FT - 1, 1)
                            if j == 9:
                                gu_hi_step(n0 + FT - 1, FT - 1, 1)
                        else:
                            if j == 4:
                                copy_part(t0 + m - 1, (m - 1) % 2, u0 + 11 * m, (m - 1) % 4)
                            if j == 6:
                                x_block(round_, m - 1, (m - 1) % 2)
                        split_hi(u0, k)

            gu_phase(0, 0, U_GU1, T_GU1)
            down_phase(1, 0, U_DOWN1, T_DOWN1, U_GU1, T_GU1)

            def head_period(ub, k0, n, p, kind, tpar):
                g, q = n - 1, 1 - p
                tile0, unit0 = T_HEADS + HEAD_TILES * n, U_HEADS + HEAD_UNITS * n
                ghost = kind == "ghost"
                for j in range(32 if ghost else HEAD_UNITS):
                    if kind != "first":
                        if j == 4:
                            act.wait_ge(arg_ready, g * 4 + 4)
                            nc.scalar.activation(decay[:, 2:4, :], decay[:, 2:4, :], ACT.Exp).then_inc(decay_ready, 1)
                            nc.scalar.activation(decay[:, 0:2, :], decay[:, 0:2, :], ACT.Exp,
                                                 scale=-1.0).then_inc(decay_ready, 1)
                            nc.scalar.activation(exp_gc[:], ps[:, 5, GC:2 * GC], ACT.Exp).then_inc(exp_gc_ready, 1)
                            nc.scalar.activation(k_tail[:], ps[:, 5, 2 * GC:3 * GC], ACT.Copy,
                                                 scale=hcol[:, q, K_TAIL:K_TAIL + 1]).then_inc(k_tail_ready, 1)
                        if j >= 7 and j % 2 == 1 and j <= 17:
                            act.wait_ge(t1_ready, g * 6 + (j - 5) // 2)
                            nc.scalar.activation(t1[:].rearrange("p a b -> p (a b)"), ps[:, 5, 0:T],
                                                 ACT.Copy).then_inc(t1_copied, 1)
                        if j == 19:
                            act.wait_ge(v0_ready, g + 1)
                            nc.scalar.activation(v_new[:, 0, :], ps[:, 6, 0:DH], ACT.Copy).then_inc(v0_copied, 1)
                        if j == 20:
                            act.wait_ge(state_ready, g + 1)
                            nc.scalar.activation(state[:], ps[:, 6, DH:2 * DH], ACT.Copy).then_inc(state_copied, 1)
                        if j == 22:
                            act.wait_ge(v1_ready, g + 1)
                            nc.scalar.activation(v_new[:, 1, :], ps[:, 6, 3 * DH:4 * DH],
                                                 ACT.Copy).then_inc(v1_copied, 1)
                        if j == 23:
                            act.wait_ge(o_ready, g + 1)
                            nc.scalar.activation(o_gdn[:], ps[:, 4, 0:T], ACT.Copy).then_inc(o_copied, 1)
                            act.wait_ge(o_copied, g + 1)
                            nc.scalar.activation(o_sq[:], o_gdn[:], ACT.Square).then_inc(o_sq_ready, 1)
                        if j == 24:
                            act.wait_ge(o_summed, g + 1)
                            nc.scalar.activation(o_sq[:], ps[:, 5, 0:T], ACT.Ln, bias=eps[:],
                                                 scale=1.0 / DH).then_inc(o_steps, 1)
                            act.wait_ge(o_steps, g * 2 + 1)
                            nc.scalar.activation(o_sq[:], o_sq[:], ACT.Exp, scale=-0.5).then_inc(o_steps, 1)
                        if j == 26:
                            act.wait_ge(y_steps, g * 2 + 2)
                            nc.scalar.activation(ya[:, g, 0:T], y_gdn[:, 1, :], ACT.Copy).then_inc(ya_hi, 1)
                        if j == 6:
                            act.wait_ge(scaled, g * HEAD_TILES + 6)
                            nc.scalar.activation(att_sq[:], att[:, 0:2, :], ACT.Square).then_inc(att_sq_ready, 1)
                        if j == 9:
                            act.wait_ge(av_turned, g + 1)
                            nc.scalar.activation(av_tok[:].rearrange("p a b -> p (a b)"), ps[:, 7, 0:T],
                                                 ACT.Copy).then_inc(av_copied, 1)
                        if j == 10:
                            act.wait_ge(att_summed, g + 1)
                            nc.scalar.activation(att_sq[:].rearrange("p a b -> p (a b)"), ps[:, 7, :], ACT.Ln,
                                                 bias=eps[:], scale=1.0 / DH).then_inc(att_steps, 1)
                            act.wait_ge(att_steps, g * 2 + 1)
                            nc.scalar.activation(att_sq[:], att_sq[:], ACT.Exp, scale=-0.5).then_inc(att_steps, 1)
                        if j == 14:
                            act.wait_ge(score_steps, g * 4 + 4)
                            nc.scalar.activation(score[:, 0:GC], score[:, 0:GC], ACT.Exp, bias=sneg[:, 0:1],
                                                 accum_out=ssum[:, 0:1]).then_inc(exp_done, 1)
                            nc.scalar.activation(score[:, GC:], score[:, GC:], ACT.Exp, bias=sneg[:, 1:2],
                                                 accum_out=ssum[:, 1:2]).then_inc(exp_done, 1)
                        if j == 16:
                            act.wait_ge(prob_turned, g + 1)
                            nc.scalar.activation(prob_t[:], ps[:, 7, 0:SCORES], ACT.Copy).then_inc(prob_copied, 1)
                        if j == 17:
                            act.wait_ge(att_o_ready, g + 1)
                            nc.scalar.activation(yb[:, g, 0:T], ps[:, 7, 0:T], ACT.Copy).then_inc(yb_hi, 1)
                    else:
                        if j == 0:
                            act.wait_ge(mix_landed, 32)
                            nc.scalar.activation(wab_hi[:], wab[:], ACT.Copy).then_inc(wab_split, 1)
                        if j == 4:
                            copy_part(T_DOWN1 + KT - 1, 1, U_HEADS, 3)
                        if j == 6:
                            x_block(1, KT - 1, 1)
                        if j == 9:
                            norm_factor(1)
                        if j == 11:
                            act.wait_ge(ab_steps, 5)
                            nc.scalar.activation(t16[:, 2, :], t16[:, 1, :], ACT.Exp, scale=-1.0).then_inc(ab_acts, 1)
                            act.wait_ge(ab_acts, 1)
                            nc.scalar.activation(t16[:, 3, :], t16[:, 2, :], ACT.Ln,
                                                 bias=const[:, C_ONES, 0:1]).then_inc(ab_acts, 1)
                            nc.scalar.activation(t16[:, 4, 0:HEADS], par[:, P_ALOG:P_ALOG + HEADS],
                                                 ACT.Exp).then_inc(ab_acts, 1)
                            nc.scalar.activation(cols[:, K_BETA:K_BETA + 2, :], ab[:, :, HEADS:],
                                                 ACT.Sigmoid).then_inc(ab_acts, 1)
                        if j == 14:
                            act.wait_ge(ab_steps, 11)
                            nc.scalar.activation(cols[:, K_EXP_GC, :], cols[:, K_GC + 1, :], ACT.Exp).then_inc(ab_acts, 1)
                            nc.scalar.activation(cols[:, K_TAIL, :], t16[:, 7, 0:HEADS], ACT.Exp).then_inc(ab_acts, 1)
                    if j % 4 == 0:
                        t = j // 4 - 2
                        if t >= 0:
                            bank = t % 4 if ghost else BANK_OF_HEAD_TILE[t]
                            copy_part(tile0 + t, (tpar + t) % 2, unit0 + 4 * (t + 1), bank)
                        elif kind != "first":
                            copy_part(tile0 + t, (tpar + t) % 2, unit0 + 4 * (t + 1),
                                      BANK_OF_HEAD_TILE[HEAD_TILES + t])
                    if j == 23 and not ghost:
                        act.wait_ge(scaled, n * HEAD_TILES + 4)
                        nc.scalar.activation(qkvz[:, p], conv[:], ACT.Silu).then_inc(silu_done, 1)
                        act.wait_ge(silu_done, n + 1)
                        nc.scalar.activation(qk_sq[:], qkvz[:, p, 0:2, :], ACT.Square).then_inc(qk_sq_ready, 1)
                    if j == 25 and not ghost:
                        act.wait_ge(qk_summed, n + 1)
                        nc.scalar.activation(qk_sq[:].rearrange("p a b -> p (a b)"), ps[:, 4, :], ACT.Ln,
                                             bias=eps[:]).then_inc(qk_steps, 1)
                        act.wait_ge(qk_steps, n * 2 + 1)
                        nc.scalar.activation(qk_sq[:], qk_sq[:], ACT.Exp, scale=-0.5).then_inc(qk_steps, 1)
                        act.wait_ge(v_turned, n + 1)
                        nc.scalar.activation(v_tok[:].rearrange("p a b -> p (a b)"), ps[:, 6, 0:T],
                                             ACT.Copy).then_inc(v_copied, 1)
                    split_hi(ub, k0 + j)

            head_period(U_HEADS, 0, 0, 0, "first", 0)
            with act.Fori(0, 3) as i:
                head_period(i * 56 + U_HEADS, 28, i * 2 + 1, 1, "", 1)
                head_period(i * 56 + U_HEADS, 56, i * 2 + 2, 0, "", 0)
            head_period(U_HEADS + 168, 28, 7, 1, "", 1)
            head_period(U_GHOST, 0, 8, 0, "ghost", 0)

            def gates_body(ub, tile0, unit0):
                for j in range(16):
                    if j % 4 == 0:
                        t = j // 4 - 2
                        copy_part(tile0 + t, t % 2, unit0 + 4 * (t + 1), t % 4)
                    split_hi(ub, j)

            with act.Fori(0, (GATES - GHOST_GATES) // 4) as i:
                gates_body(i * 16 + U_GATES, i * 4 + (T_GHOST + GHOST_GATES), i * 16 + U_GATES)

            def branch_tile(m, m4):
                copy_part(m + T_BRANCH, m4 % 2, m * 4 + (U_BRANCH + 4), 2 * m4, pair=True)
                if not (isinstance(m, int) and m < 2):
                    act.wait_ge(branch_steps, m * 2 - 2)
                else:
                    act.wait_ge(scaled, HEADS * HEAD_TILES + GATES)
                nc.scalar.activation(sig[:, m4 % 2], gates[:, bass.ds(m * 2, 2), :], ACT.Sigmoid).then_inc(sig_ready, 1)

            def branch_hi(m, s):
                act.wait_ge(branch_steps, m * 2 + 2)
                nc.scalar.activation(mixed[:, m, 0:T], mixed_f[:, s, :], ACT.Copy).then_inc(mixed_hi, 1)

            def branch_body(ub, m0, first):
                for j in range(16):
                    t = j // 4 - 2
                    if j % 4 == 0:
                        if first and t < 0:
                            tile = T_BRANCH + t
                            copy_part(tile, t % 2, U_BRANCH + 4 * (t + 1), t % 4)
                        else:
                            branch_tile(m0 + t, t % 4)
                    if j % 4 == 2 and not (first and t < 1):
                        branch_hi(m0 + (t - 1), (t - 1) % 2)
                    split_hi(ub, j)

            branch_body(U_BRANCH, 0, True)
            with act.Fori(1, 4) as i:
                branch_body(i * 16 + U_BRANCH, i * 4, False)

            def out_body(ub, m0, first):
                for j in range(16):
                    t = j // 4 - 2
                    if first and t < 0:
                        if j % 4 == 0:
                            branch_tile(KT + t, t % 4)
                        if j in (2, 6, 7):
                            b = {2: 13, 6: 14, 7: 15}[j]
                            branch_hi(b, b % 2)
                    else:
                        if j % 4 == 0:
                            copy_part(m0 + (T_OUT + t), t % 2, m0 * 4 + (U_OUT + 4 * (t + 1)), t % 4)
                        if j % 4 == 2:
                            x_block(2, m0 + t, t % 2)
                    split_hi(ub, j)

            out_body(U_OUT, 0, True)
            with act.Fori(1, 4) as i:
                out_body(i * 16 + U_OUT, i * 4, False)

            gu_phase(2, FT, U_GU2, T_GU2)
            down_phase(3, FT, U_DOWN2, T_DOWN2, U_GU2, T_GU2)

            for j in range(8):
                if j == 0:
                    act.wait_ge(p_landed, 16)
                    nc.scalar.activation(p_hl[:, :, 0:T], p_raw[:], ACT.Copy).then_inc(p_hi, 1)
                if j == 4:
                    copy_part(T_DOWN2 + KT - 1, 1, U_PROJ, 3)
                if j == 6:
                    x_block(3, KT - 1, 1)
                if j >= 5:
                    copy_part(T_PROJ + j - 5, (j - 5) % 2, U_PROJ + j - 4, 2 * ((j - 5) % 2), pair=True)
                split_hi(U_PROJ, j)

            def ple_sig_step(m, s):
                act.wait_ge(ple_scaled, m + 1)
                nc.scalar.activation(act2[:, s, :], gate_s[:, s, :], ACT.Sigmoid).then_inc(ple_sig, 1)

            def store(i):
                act.wait_ge(y_parts, i * 8 + 8)
                act.dma_start(y_out[i], y[:, bass.ds(i * 4, 4), :]).then_inc(y_stored, 16)

            def ple_body(ub, i, first):
                for j in range(16):
                    t = j // 4 - 2
                    if first and j < 5:
                        b = j + 3
                        copy_part(T_PROJ + b, b % 2, U_PROJ + b + 1, 2 * (b % 2), pair=True)
                        if j == 2:
                            norm_factor(3)
                    if not (first and t < 0):
                        if j % 4 == 0:
                            copy_part(i * 4 + (T_PLE + t), t % 2, i * 16 + (U_PLE + 4 * (t + 1)), t % 4)
                        if j % 4 == 3:
                            ple_sig_step(i * 4 + t, t % 2)
                        if j == 14 and not first:
                            store(i - 1)
                    split_hi(ub, j)

            ple_body(U_PLE, 0, True)
            with act.Fori(1, 4) as i:
                ple_body(i * 16 + U_PLE, i, False)
            for m in (14, 15):
                copy_part(T_PLE + m, m % 2, U_PLE + 4 * (m + 1), m % 4)
                ple_sig_step(m, m % 2)
            store(3)
            act.wait_ge(y_stored, 16 * 4)

        @block.vector
        def _(dve):
            def split_lo(ub, k):
                dve.wait_ge(hi_ready, ub + (k + 1))
                nc.vector.tensor_tensor(w_lo[:, k % HL, :], raw[:, k % RAW, :], w_hi[:, k % HL, :].bitcast(F32),
                                        ALU.subtract).then_inc(lo_ready, 1)

            def add_parts(tile, par_, bank, out=None, pair=False):
                dve.wait_ge(part_ready, tile + 1)
                if pair:
                    if out is None:
                        out = whole[:, par_, :].rearrange("p (a b) -> p a b", a=2)
                    nc.vector.tensor_tensor(out, ps[:, bank:bank + 2, 0:T],
                                            part[:, par_, :].rearrange("p (a b) -> p a b", a=2),
                                            ALU.add).then_inc(tile_free, 1)
                else:
                    nc.vector.tensor_tensor(whole[:, par_, 0:T], ps[:, bank, 0:T], part[:, par_, 0:T],
                                            ALU.add).then_inc(tile_free, 1)

            def x_update(round_, tile, m, par_, bank, half):
                add_parts(tile, par_, bank)
                dve.wait_ge(tile_free, tile + 1)
                if half:
                    ins = nc.vector.scalar_tensor_tensor(out=x[:, m, :], in0=whole[:, par_, 0:T], scalar=0.5,
                                                         in1=x[:, m, :], op0=ALU.mult, op1=ALU.add)
                else:
                    ins = nc.vector.tensor_tensor(x[:, m, :], whole[:, par_, 0:T], x[:, m, :], ALU.add)
                ins.then_inc(x_new, 1)

            def acc_add(round_, m, s):
                dve.wait_ge(xw_hi, m + (KT * round_ + 1))
                nc.vector.scalar_tensor_tensor(out=xw[:, m, T:], in0=x[:, m, :],
                                               scalar=par[:, bass.ds(m + (P_NORMS + KT * round_), 1)],
                                               in1=xw[:, m, 0:T].bitcast(F32), op0=ALU.mult,
                                               op1=ALU.subtract).then_inc(xw_lo, 1)
                dve.wait_ge(xsq_ready, m + (KT * round_ + 1))
                if isinstance(m, int) and m == 0:
                    if round_ > 0:
                        dve.wait_ge(norm_summed, round_)
                    nc.vector.tensor_copy(acc[:], xsq[:, s, :]).then_inc(acc_added, 1)
                else:
                    dve.wait_ge(acc_added, m + KT * round_)
                    nc.vector.tensor_tensor(acc[:], acc[:], xsq[:, s, :], ALU.add).then_inc(acc_added, 1)

            dve.wait_ge(par_landed, 16)
            nc.vector.memset(eps[:], EPS).then_inc(eps_set, 1)
            for m in range(KT):
                acc_add(0, m, m % 2)
                if m % 4 == 3:
                    split_lo(0, m // 4)

            def gu_add(n, tile, p):
                add_parts(tile, p, 2 * p, pair=True)
                dve.wait_ge(tile_free, tile + 1)
                w2 = whole[:, p, :].rearrange("p (a b) -> p a b", a=2)
                nc.vector.tensor_tensor(w2, w2, both(r[:]), ALU.mult).then_inc(gu_scaled, 1)

            def gu_product(n, p):
                dve.wait_ge(gu_silu, n + 1)
                dve.wait_ge(hid_lo, n + 1)
                nc.vector.tensor_tensor(prod[:, p, :], act2[:, p, :], whole[:, p, T:], ALU.mult).then_inc(hid_new, 1)

            def out_tail(j):
                m = 14 + j // 4
                if j % 4 == 1:
                    x_update(2, T_OUT + m, m, m % 2, m % 4, False)
                if j % 4 == 3:
                    acc_add(2, m, m % 2)

            def gu_tile(ub, k0, n0, f, p, t0, first, older):
                for j in range(8):
                    if j == 0 and older:
                        gu_product(n0 + f - 2, p)
                    if n0 == FT and first and k0 == 0:
                        out_tail(j)
                    if j == 5 and (not first or k0 > 0):
                        if first:
                            dve.wait_ge(r_ready, first)
                        gu_add(n0 + f - 1, t0 + f - 1, 1 - p)
                    if not (first == 1 and k0 + j < 4):
                        split_lo(ub, k0 + j)

            def gu_phase(round_, n0, u0, t0):
                gu_tile(u0, 0, n0, 0, 0, t0, round_ + 1, False)
                gu_tile(u0, 8, n0, 1, 1, t0, round_ + 1, False)
                with dve.Fori(1, FT // 2) as i:
                    gu_tile(i * 16 + u0, 0, n0, i * 2, 0, t0, 0, True)
                    gu_tile(i * 16 + u0, 8, n0, i * 2 + 1, 1, t0, 0, True)

            def down_phase(round_, n0, u0, t0, gu_t):
                for m in range(KT):
                    for j in range(11):
                        k = 11 * m + j
                        if m == 0:
                            if j == 0:
                                gu_product(n0 + FT - 2, 0)
                            if j == 5:
                                gu_add(n0 + FT - 1, gu_t + FT - 1, 1)
                            if j == 8:
                                gu_product(n0 + FT - 1, 1)
                        else:
                            if j == 5:
                                x_update(round_, t0 + m - 1, m - 1, (m - 1) % 2, (m - 1) % 4, True)
                            if j == 7:
                                acc_add(round_, m - 1, (m - 1) % 2)
                        split_lo(u0, k)

            gu_phase(0, 0, U_GU1, T_GU1)
            down_phase(1, 0, U_DOWN1, T_DOWN1, T_GU1)

            def head_period(ub, k0, n, p, kind, tpar):
                g, q = n - 1, 1 - p
                tile0 = T_HEADS + HEAD_TILES * n
                ghost = kind == "ghost"
                col = lambda i: hcol[:, q, i:i + 1]
                for j in range(32 if ghost else HEAD_UNITS):
                    if kind != "first":
                        if j == 4:
                            dve.wait_ge(gc_ready, g + 1)
                            for c in range(2):
                                nc.vector.tensor_scalar(decay[:, 2 + c, :], ps[:, 5, c * GC:(c + 1) * GC], col(K_GC + c),
                                                        0.0, ALU.subtract, ALU.min).then_inc(arg_ready, 1)
                            for c in range(2):
                                nc.vector.tensor_scalar(decay[:, c, :], ps[:, 5, c * GC:(c + 1) * GC], col(K_GC + c),
                                                        0.0, ALU.subtract, ALU.max).then_inc(arg_ready, 1)
                        if j == 5:
                            dve.wait_ge(decay_ready, g * 2 + 2)
                            dve.wait_ge(gram_ready, g + 1)
                            for c in range(2):
                                nc.vector.scalar_tensor_tensor(
                                    out=lmat[:, c, :], in0=ps[:, 4, c * GC:(c + 1) * GC], scalar=col(K_BETA + c),
                                    in1=decay[:, c, :], op0=ALU.mult, op1=ALU.mult).then_inc(lmat_ready, 1)
                            nc.vector.tensor_scalar(rhs0[:], v_tok[:, 0, :], col(K_BETA), None,
                                                    ALU.mult).then_inc(rhs0_ready, 1)
                            dve.wait_ge(exp_gc_ready, g + 1)
                            nc.vector.tensor_tensor(qe[:], qn[:, GC:], exp_gc[:], ALU.mult).then_inc(qe_ready, 1)
                        if j == 6:
                            dve.wait_ge(incl_ready, g + 1)
                            nc.vector.tensor_tensor(a_qk[:].rearrange("p a b -> p (a b)"), ps[:, 4, 2 * GC:],
                                                    decay[:, 2:4, :].rearrange("p a b -> p (a b)"),
                                                    ALU.mult).then_inc(a_qk_ready, 1)
                            dve.wait_ge(c0_turned, g + 1)
                            nc.vector.tensor_tensor(inv[:, 2:4, :], both(ident),
                                                    ps[:, 5, 0:T].rearrange("p (a b) -> p a b", a=2), ALU.subtract)
                            nc.vector.tensor_tensor(inv[:, 0:2, :], both(ident), cmat[:, 0],
                                                    ALU.subtract).then_inc(inv_ready, 1)
                        if j >= 8 and j % 2 == 0 and j <= 18:
                            s = (j - 6) // 2
                            dve.wait_ge(step_ready, g * 6 + s)
                            dve.wait_ge(inv_ready, g * LEVELS + s)
                            lo = 0 if s < 6 else 2
                            nc.vector.tensor_tensor(inv[:, lo:4, :].rearrange("p a b -> p (a b)"),
                                                    inv[:, lo:4, :].rearrange("p a b -> p (a b)"),
                                                    ps[:, 4, lo * GC:], ALU.subtract).then_inc(inv_ready, 1)
                        if j == 21:
                            dve.wait_ge(ks_ready, g + 1)
                            nc.vector.scalar_tensor_tensor(out=rhs1[:, 0, :], in0=ps[:, 6, 2 * DH:3 * DH],
                                                           scalar=col(K_EXP_GC), in1=v_tok[:, 1, :], op0=ALU.mult,
                                                           op1=ALU.subtract).then_inc(rhs1_steps, 1)
                            dve.wait_ge(rhs1_steps, g * 2 + 1)
                            nc.vector.tensor_scalar(rhs1[:, 1, :], rhs1[:, 0, :], col(K_NEG_BETA), None,
                                                    ALU.mult).then_inc(rhs1_steps, 1)
                        if j == 25:
                            dve.wait_ge(o_steps, g * 2 + 2)
                            nc.vector.scalar_tensor_tensor(out=y_gdn[:, 0, :], in0=o_gdn[:],
                                                           scalar=par[:, P_GDN_NORM:P_GDN_NORM + 1], in1=o_sq[:],
                                                           op0=ALU.mult, op1=ALU.mult).then_inc(y_steps, 1)
                            dve.wait_ge(y_steps, g * 2 + 1)
                            dve.wait_ge(scaled, g * HEAD_TILES + 6)
                            nc.vector.tensor_tensor(y_gdn[:, 1, :], y_gdn[:, 0, :], qkvz[:, q, 3, :],
                                                    ALU.mult).then_inc(y_steps, 1)
                        if j == 11:
                            dve.wait_ge(att_steps, g * 2 + 2)
                            for i in range(2):
                                nc.vector.scalar_tensor_tensor(
                                    out=att_n[:, i, :], in0=att[:, i, :], scalar=par[:, P_Q_NORM + i:P_Q_NORM + i + 1],
                                    in1=att_sq[:, i, :], op0=ALU.mult, op1=ALU.mult).then_inc(att_normed, 1)
                        if j == 13:
                            dve.wait_ge(score_ready, g + 1)
                            nc.vector.scalar_tensor_tensor(out=score[:], in0=ps[:, 7, 0:SCORES], scalar=DH ** -0.5,
                                                           in1=bias[:, g, :], op0=ALU.mult,
                                                           op1=ALU.add).then_inc(score_steps, 1)
                            dve.wait_ge(score_steps, g * 4 + 1)
                            nc.vector.tensor_reduce(smax[:, 0:1], score[:, 0:GC], AX.X, ALU.max).then_inc(score_steps, 1)
                            nc.vector.tensor_reduce(smax[:, 1:2], score[:, GC:], AX.X, ALU.max).then_inc(score_steps, 1)
                            dve.wait_ge(score_steps, g * 4 + 3)
                            nc.vector.tensor_scalar(sneg[:], smax[:], -1.0, None, ALU.mult).then_inc(score_steps, 1)
                        if j == 15:
                            dve.wait_ge(exp_done, g * 2 + 2)
                            nc.vector.reciprocal(sinv[:], ssum[:]).then_inc(sinv_ready, 1)
                            dve.wait_ge(sinv_ready, g + 1)
                            nc.vector.tensor_scalar(score[:, 0:GC], score[:, 0:GC], sinv[:, 0:1], None,
                                                    ALU.mult).then_inc(prob_ready, 1)
                            nc.vector.tensor_scalar(score[:, GC:], score[:, GC:], sinv[:, 1:2], None,
                                                    ALU.mult).then_inc(prob_ready, 1)
                        if j == 18:
                            dve.wait_ge(yb_hi, g + 1)
                            nc.vector.tensor_tensor(yb[:, g, T:], ps[:, 7, 0:T], yb[:, g, 0:T].bitcast(F32),
                                                    ALU.subtract).then_inc(yb_lo, 1)
                    else:
                        if j == 0:
                            dve.wait_ge(wab_split, 1)
                            nc.vector.tensor_tensor(wab_lo[:], wab[:], wab_hi[:].bitcast(F32),
                                                    ALU.subtract).then_inc(wab_lo_ready, 1)
                        if j == 5:
                            x_update(1, T_DOWN1 + KT - 1, KT - 1, 1, 3, True)
                        if j == 7:
                            acc_add(1, KT - 1, 1)
                        if j == 10:
                            dve.wait_ge(ab_ready, 1)
                            nc.vector.tensor_copy(r_tok[:], ps[:, 5, 32:34]).then_inc(ab_steps, 1)
                            dve.wait_ge(ab_steps, 1)
                            for c in range(2):
                                ins = nc.vector.tensor_scalar(ab[:, c, :], ps[:, 5, 16 * c:16 * c + 16],
                                                              r_tok[:, c:c + 1], None, ALU.mult)
                            ins.then_inc(ab_steps, 1)
                            dve.wait_ge(ab_steps, 2)
                            a_dt = t16[:, 0, :].rearrange("p (a b) -> p a b", a=2)
                            nc.vector.tensor_tensor(a_dt, ab[:, :, 0:HEADS], both(par[:, P_DT:P_DT + HEADS]),
                                                    ALU.add).then_inc(ab_steps, 1)
                            dve.wait_ge(ab_steps, 3)
                            nc.vector.tensor_scalar(t16[:, 5, :], t16[:, 0, :], -1.0, None, ALU.mult).then_inc(ab_steps, 1)
                            dve.wait_ge(ab_steps, 4)
                            nc.vector.tensor_tensor(t16[:, 1, :], t16[:, 0, :], t16[:, 5, :], ALU.max).then_inc(ab_steps, 1)
                        if j == 12:
                            dve.wait_ge(ab_acts, 4)
                            nc.vector.scalar_tensor_tensor(out=t16[:, 6, :], in0=t16[:, 0, :], scalar=0.0,
                                                           in1=t16[:, 3, :], op0=ALU.max,
                                                           op1=ALU.add).then_inc(ab_steps, 1)
                            dve.wait_ge(ab_steps, 6)
                            nc.vector.scalar_tensor_tensor(
                                out=cols[:, K_G:K_G + 2, :], in0=t16[:, 6, :].rearrange("p (a b) -> p a b", a=2),
                                scalar=-1.0, in1=both(t16[:, 4, 0:HEADS]), op0=ALU.mult,
                                op1=ALU.mult).then_inc(ab_steps, 1)
                            nc.vector.tensor_scalar(cols[:, K_NEG_BETA, :], cols[:, K_BETA + 1, :], -1.0, None,
                                                    ALU.mult).then_inc(ab_steps, 1)
                        if j == 13:
                            dve.wait_ge(gc_summed, 1)
                            nc.vector.tensor_copy(cols[:, K_GC:K_GC + 2, :],
                                                  ps[:, 5, 64:80].rearrange("p (a b) -> p a b", a=2)
                                                  ).then_inc(ab_steps, 1)
                            dve.wait_ge(ab_steps, 9)
                            nc.vector.tensor_tensor(t16[:, 7, 0:HEADS], ps[:, 5, 80:88], cols[:, K_GC, :],
                                                    ALU.subtract).then_inc(ab_steps, 2)
                    if j % 4 == 1:
                        t = j // 4 - 2
                        if t >= 0:
                            bank = t % 4 if ghost else BANK_OF_HEAD_TILE[t]
                        else:
                            bank = BANK_OF_HEAD_TILE[HEAD_TILES + t]
                        if t >= 0 or kind != "first":
                            if kind == "first" and t < 2:
                                pass
                            else:
                                dve.wait_ge(scaled, n * HEAD_TILES + (t - 1))
                            add_parts(tile0 + t, (tpar + t) % 2, bank)
                    if j == 26 and not ghost:
                        dve.wait_ge(qk_steps, n * 2 + 2)
                        nc.vector.tensor_tensor(kn[:], qkvz[:, p, 1, :], qk_sq[:, 1, :], ALU.mult).then_inc(qk_normed, 1)
                        nc.vector.scalar_tensor_tensor(out=qn[:], in0=qkvz[:, p, 0, :], scalar=DH ** -0.5,
                                                       in1=qk_sq[:, 0, :], op0=ALU.mult,
                                                       op1=ALU.mult).then_inc(qk_normed, 1)
                    if j == 27 and not ghost:
                        if kind == "first":
                            dve.wait_ge(ab_acts, 6)
                        nc.vector.tensor_copy(hcol[:, p, :], cols[:, :, n]).then_inc(hcol_ready, 1)
                        dve.wait_ge(hcol_ready, n + 1)
                        for c in range(2):
                            nc.vector.tensor_scalar(upper_g[:, c, :], upper, hcol[:, p, K_G + c:K_G + c + 1], None,
                                                    ALU.mult).then_inc(upper_ready, 1)
                    split_lo(ub, k0 + j)

            head_period(U_HEADS, 0, 0, 0, "first", 0)
            with dve.Fori(0, 3) as i:
                head_period(i * 56 + U_HEADS, 28, i * 2 + 1, 1, "", 1)
                head_period(i * 56 + U_HEADS, 56, i * 2 + 2, 0, "", 0)
            head_period(U_HEADS + 168, 28, 7, 1, "", 1)
            head_period(U_GHOST, 0, 8, 0, "ghost", 0)

            with dve.Fori(0, (GATES - GHOST_GATES) // 4) as i:
                for j in range(16):
                    if j % 4 == 1:
                        t = j // 4 - 2
                        dve.wait_ge(scaled, i * 4 + (HEADS * HEAD_TILES + GHOST_GATES + t - 1))
                        add_parts(i * 4 + (T_GHOST + GHOST_GATES + t), t % 2, t % 4)
                    split_lo(i * 16 + U_GATES, j)

            def branch_add(m, m4):
                if not (isinstance(m, int) and m < 2):
                    dve.wait_ge(branch_steps, m * 2 - 2)
                add_parts(m + T_BRANCH, m4 % 2, 2 * m4, pair=True)

            def branch_body(ub, m0, first):
                for j in range(16):
                    t = j // 4 - 2
                    if j % 4 == 1:
                        if first and t < 0:
                            dve.wait_ge(scaled, HEADS * HEAD_TILES + GATES + t - 1)
                            add_parts(T_BRANCH + t, t % 2, t % 4)
                        else:
                            if first and t == 0:
                                dve.wait_ge(scaled, HEADS * HEAD_TILES + GATES)
                            branch_add(m0 + t, t % 4)
                    split_lo(ub, j)

            branch_body(U_BRANCH, 0, True)
            with dve.Fori(1, 4) as i:
                branch_body(i * 16 + U_BRANCH, i * 4, False)

            def out_body(ub, m0, first):
                for j in range(16):
                    t = j // 4 - 2
                    if first and t < 0:
                        if j % 4 == 1:
                            branch_add(KT + t, t % 4)
                    else:
                        if j % 4 == 1:
                            if first:
                                dve.wait_ge(branch_steps, 2 * KT)
                            x_update(2, m0 + (T_OUT + t), m0 + t, t % 2, t % 4, False)
                        if j % 4 == 3:
                            acc_add(2, m0 + t, t % 2)
                    split_lo(ub, j)

            out_body(U_OUT, 0, True)
            with dve.Fori(1, 4) as i:
                out_body(i * 16 + U_OUT, i * 4, False)

            gu_phase(2, FT, U_GU2, T_GU2)
            down_phase(3, FT, U_DOWN2, T_DOWN2, T_GU2)

            for j in range(8):
                if j == 0:
                    dve.wait_ge(p_hi, 1)
                    nc.vector.tensor_tensor(p_hl[:, :, T:], p_raw[:], p_hl[:, :, 0:T].bitcast(F32),
                                            ALU.subtract).then_inc(p_lo, 1)
                if j == 5:
                    x_update(3, T_DOWN2 + KT - 1, KT - 1, 1, 3, True)
                if j == 7:
                    acc_add(3, KT - 1, 1)
                if j >= 6:
                    add_parts(T_PROJ + j - 6, (j - 6) % 2, 2 * ((j - 6) % 2), emb[:, 2 * (j - 6):2 * (j - 5), :], pair=True)
                split_lo(U_PROJ, j)

            def ple_add(m, s, bank):
                if not (isinstance(m, int) and m < 2):
                    dve.wait_ge(ple_scaled, m - 1)
                add_parts(m + T_PLE, s, bank)

            def ple_y(m, s):
                dve.wait_ge(ple_sig, m + 1)
                nc.vector.tensor_tensor(prod[:, s, :], act2[:, s, :], emb[:, m, :], ALU.mult).then_inc(y_parts, 1)
                dve.wait_ge(y_parts, m * 2 + 1)
                nc.vector.tensor_tensor(y[:, m, :], prod[:, s, :], x[:, m, :], ALU.add).then_inc(y_parts, 1)

            def ple_body(ub, m0, first):
                for j in range(16):
                    t = j // 4 - 2
                    if first and j < 6:
                        b = j + 2
                        add_parts(T_PROJ + b, b % 2, 2 * (b % 2), emb[:, 2 * b:2 * b + 2, :], pair=True)
                    if j % 4 == 1 and not (first and t < 0):
                        ple_add(m0 + t, t % 2, t % 4)
                    if j % 4 == 0 and not (first and t < 1):
                        ple_y(m0 + (t - 1), (t - 1) % 2)
                    split_lo(ub, j)

            ple_body(U_PLE, 0, True)
            with dve.Fori(1, 4) as i:
                ple_body(i * 16 + U_PLE, i * 4, False)
            ple_y(13, 1)
            for m in (14, 15):
                ple_add(m, m % 2, m % 4)
                ple_y(m, m % 2)

        @block.gpsimd
        def _(pool):
            def hidden_lo(n, f, p):
                pool.wait_ge(hid_hi, n + 1)
                nc.gpsimd.tensor_tensor(hid[:, f, T:], prod[:, p, :], hid[:, f, 0:T].bitcast(F32),
                                        ALU.subtract).then_inc(hid_lo, 1)

            nc.gpsimd.memset(unread[:], 0.0).then_inc(hid_lo, 2)
            with pool.Fori(0, FT // 2) as i:
                for p in range(2):
                    hidden_lo(i * 2 + p, i * 2 + p, p)

            pool.wait_ge(unit_used, U_HEADS)
            nc.gpsimd.memset(padded[:], 0.0).then_inc(pad_zero, 1)
            pool.wait_ge(pad_zero, 1)
            pool.wait_ge(r_ready, 2)

            def scale_tile(n, t, s, out):
                pool.wait_ge(tile_free, n * HEAD_TILES + (T_HEADS + t + 1))
                nc.gpsimd.tensor_tensor(out, whole[:, s, 0:T], r[:], ALU.mult).then_inc(scaled, 1)

            def causal_conv(n, c):
                pool.wait_ge(scaled, n * HEAD_TILES + (c + 1))
                w = lambda i: taps[:, c * CONV_K + i:c * CONV_K + i + 1]
                for i in range(CONV_K):
                    if not (isinstance(n, int) and n == 0 and c == 0 and i == 0):
                        pool.wait_ge(conv_steps, n * (6 * CONV_K) + (2 * (c * CONV_K + i)))
                    nc.gpsimd.tensor_tensor(conv[:, c, :] if i == 0 else tap[:], padded[:, c, i:i + T],
                                            w(i).to_broadcast([P, T]), ALU.mult).then_inc(conv_steps, 1 if i else 2)
                    if i:
                        pool.wait_ge(conv_steps, n * (6 * CONV_K) + (2 * (c * CONV_K + i) + 1))
                        nc.gpsimd.tensor_tensor(conv[:, c, :], conv[:, c, :], tap[:], ALU.add).then_inc(conv_steps, 1)

            def head_period(n, p, kind, tpar):
                g = n - 1
                if kind != "first":
                    scale_tile(g, 5, (tpar - 2) % 2, att[:, 1, :])
                    pool.wait_ge(decay_ready, g * 2 + 1)
                    nc.gpsimd.tensor_tensor(decay[:, 2:4, :], decay[:, 2:4, :], both(upper),
                                            ALU.mult).then_inc(incl_ready, 1)
                    pool.wait_ge(lmat_ready, g * 2 + 2)
                    nc.gpsimd.tensor_tensor(cmat[:, 0], lmat[:], both(const[:, C_MASKS, :]),
                                            ALU.mult).then_inc(cmat_ready, 1)
                    scale_tile(g, 6, (tpar - 1) % 2, att[:, 2, :])
                    for s in range(1, LEVELS):
                        nc.gpsimd.tensor_tensor(cmat[:, s], lmat[:], both(const[:, C_MASKS + s, :]),
                                                ALU.mult).then_inc(cmat_ready, 1)
                if kind != "ghost":
                    if kind != "first":
                        pool.wait_ge(silu_done, n)
                    nc.gpsimd.tensor_copy(taps[:], par[:, bass.ds(n * (3 * CONV_K) + P_CONV, 3 * CONV_K)]
                                          ).then_inc(taps_ready, 1)
                    pool.wait_ge(taps_ready, n + 1)
                    for c in range(3):
                        scale_tile(n, c, (tpar + c) % 2, padded[:, c, CONV_K - 1:])
                        causal_conv(n, c)
                    scale_tile(n, 3, (tpar + 3) % 2, conv[:, 3, :])
                    if kind != "first":
                        pool.wait_ge(att_normed, g * 2 + 2)
                    scale_tile(n, 4, (tpar + 4) % 2, att[:, 0, :])
                else:
                    for t in range(GHOST_GATES - 2):
                        scale_tile(n, t, t % 2, gates[:, t, :])
                if kind != "first":
                    pool.wait_ge(ya_hi, g + 1)
                    nc.gpsimd.tensor_tensor(ya[:, g, T:], y_gdn[:, 1, :], ya[:, g, 0:T].bitcast(F32),
                                            ALU.subtract).then_inc(ya_lo, 1)

            head_period(0, 0, "first", 0)
            with pool.Fori(0, 3) as i:
                head_period(i * 2 + 1, 1, "", 1)
                head_period(i * 2 + 2, 0, "", 0)
            head_period(7, 1, "", 1)
            head_period(8, 0, "ghost", 0)

            pool.wait_ge(yb_lo, HEADS)
            with pool.Fori(0, (GATES - GHOST_GATES + 2) // 2) as i:
                for s in range(2):
                    pool.wait_ge(tile_free, i * 2 + (T_GHOST + GHOST_GATES - 2 + s + 1))
                    nc.gpsimd.tensor_tensor(gates[:, i * 2 + (GHOST_GATES - 2 + s), :], whole[:, s, 0:T], r[:],
                                            ALU.mult).then_inc(scaled, 1)

            def branch_mix(m, s, first):
                pool.wait_ge(sig_ready, m + 1)
                pool.wait_ge(tile_free, m + (T_BRANCH + 1))
                w2 = whole[:, s, :].rearrange("p (a b) -> p a b", a=2)
                nc.gpsimd.tensor_tensor(w2, w2, sig[:, s], ALU.mult).then_inc(branch_steps, 1)
                pool.wait_ge(branch_steps, m * 2 + 1)
                if not first:
                    pool.wait_ge(mixed_lo, m - 1)
                nc.gpsimd.tensor_tensor(mixed_f[:, s, :], whole[:, s, 0:T], whole[:, s, T:],
                                        ALU.add).then_inc(branch_steps, 1)

            def mixed_lo_step(m, s):
                pool.wait_ge(mixed_hi, m + 1)
                nc.gpsimd.tensor_tensor(mixed[:, m, T:], mixed_f[:, s, :], mixed[:, m, 0:T].bitcast(F32),
                                        ALU.subtract).then_inc(mixed_lo, 1)

            branch_mix(0, 0, True)
            branch_mix(1, 1, True)
            mixed_lo_step(0, 0)
            with pool.Fori(1, KT // 2) as i:
                branch_mix(i * 2, 0, False)
                mixed_lo_step(i * 2 - 1, 1)
                branch_mix(i * 2 + 1, 1, False)
                mixed_lo_step(i * 2, 0)
            mixed_lo_step(KT - 1, 1)

            with pool.Fori(FT // 2, FT) as i:
                for p in range(2):
                    hidden_lo(i * 2 + p, i * 2 - FT + p, p)

            with pool.Fori(0, KT // 2) as i:
                pool.wait_ge(r_ready, 4)
                for s in range(2):
                    pool.wait_ge(tile_free, i * 2 + (T_PLE + s + 1))
                    nc.gpsimd.tensor_tensor(gate_s[:, s, :], whole[:, s, 0:T], r[:], ALU.mult).then_inc(ple_scaled, 1)

        @block.tensor
        def _(pe):
            def unit(ub, k, tile_k, n_k, bank, rhs, visit=None):
                pe.wait_ge(lo_ready, ub + (k + 1))
                for i in range(UK):
                    kt = tile_k + i
                    hi, lo = (w[:, k % HL, i * P:(i + 1) * P] for w in (w_hi, w_lo))
                    whole_mm = lambda: nc.tensor.matmul(ps[:, bank, :], hi, rhs(kt),
                                                        start=(kt == 0), stop=(kt == n_k - 1))
                    half_mm = lambda: nc.tensor.matmul(ps[:, bank, 0:T], lo, rhs(kt)[:, 0:T],
                                                       start=False, stop=False)
                    if kt == 0:
                        whole_mm()
                        last = half_mm()
                    else:
                        half_mm()
                        last = whole_mm()
                last.then_inc(unit_used, 1)

            def from_x(kt):
                return xw[:, kt, :]

            def norm_visit(round_):
                pe.wait_ge(const_landed, 16)
                pe.wait_ge(acc_added, KT * (round_ + 1))
                nc.tensor.matmul(ps[:, 4, 0:T], ones, acc[:], start=True, stop=True).then_inc(norm_summed, 1)

            def gu_tile(ub, k0, tile, p, first):
                if not first:
                    pe.wait_ge(tile_free, tile - 1)
                for j in range(8):
                    if first and first != 5 and k0 == 0 and j < 4:
                        for kt in range(4 * j, 4 * j + 4):
                            pe.wait_ge(xw_lo, KT * (first - 1) + kt + 1)
                    unit(ub, k0 + j, 4 * (j % 4), KT, 2 * p + j // 4, from_x)
                    if first and k0 == 0 and j == 5:
                        norm_visit(first - 1)

            def gu_phase(round_, u0, t0):
                if round_:
                    pe.wait_ge(tile_free, t0 - 2)
                gu_tile(u0, 0, t0, 0, round_ + 1)
                if round_:
                    pe.wait_ge(tile_free, t0)
                gu_tile(u0, 8, t0 + 1, 1, round_ + 1)
                with pe.Fori(1, FT // 2) as i:
                    gu_tile(i * 16 + u0, 0, i * 2 + t0, 0, 0)
                    gu_tile(i * 16 + u0, 8, i * 2 + (t0 + 1), 1, 0)

            def down_phase(n0, u0, t0):
                for m in range(KT):
                    pe.wait_ge(tile_free, t0 + m - (1 if m == 0 else 2))
                    for j in range(11):
                        if m == 0:
                            if j == 0:
                                pe.wait_ge(hid_lo, n0 + FT)
                            if j == 10:
                                pe.wait_ge(hid_lo, n0 + FT + 2)
                        unit(u0, 11 * m + j, 4 * j, FT, m % 4, lambda kt: hid[:, kt, :])

            gu_phase(0, U_GU1, T_GU1)
            down_phase(0, U_DOWN1, T_DOWN1)

            def head_period(ub, k0, n, p, kind):
                g, q = n - 1, 1 - p
                tile0 = T_HEADS + HEAD_TILES * n
                ghost = kind == "ghost"
                for j in range(32 if ghost else HEAD_UNITS):
                    t = j // 4
                    if j % 4 == 0:
                        pe.wait_ge(tile_free, tile0 + (t - 2))
                    if kind == "first" and j < 4:
                        pe.wait_ge(xw_lo, KT + 4 * j + 4)
                    unit(ub, k0 + j, 4 * (j % 4), KT, t % 4 if ghost else BANK_OF_HEAD_TILE[t], from_x)
                    if kind == "first":
                        if j == 5:
                            norm_visit(1)
                        if j == 6:
                            pe.wait_ge(wab_lo_ready, 1)
                            pe.wait_ge(r_ready, 2)
                            for c in range(2):
                                out = ps[:, 5, 16 * c:16 * c + 16]
                                for kt in range(KT):
                                    x_h, x_l = (xw[:, kt, o + c * GC:o + (c + 1) * GC] for o in (0, T))
                                    w_h, w_l = (w[:, kt * 16:kt * 16 + 16] for w in (wab_hi, wab_lo))
                                    nc.tensor.matmul(out, x_h, w_h, start=(kt == 0), stop=False)
                                    nc.tensor.matmul(out, x_l, w_h, start=False, stop=False)
                                    nc.tensor.matmul(out, x_h, w_l, start=False, stop=(kt == KT - 1))
                            for c in range(2):
                                last = nc.tensor.matmul(ps[:, 5, 32 + c:33 + c], r[0:1, c * GC:(c + 1) * GC],
                                                        const[0:1, C_ONES, 0:1], start=True, stop=True)
                            last.then_inc(ab_ready, 1)
                        if j == 9:
                            pe.wait_ge(ab_steps, 8)
                            g_all = cols[:, K_G:K_G + 2, :].rearrange("p a b -> p (a b)")
                            nc.tensor.matmul(ps[:, 5, 64:80], upper, g_all, start=True, stop=True)
                            nc.tensor.matmul(ps[:, 5, 80:96], ones, g_all, start=True, stop=True).then_inc(gc_summed, 1)
                    else:
                        if j == 0:
                            pe.wait_ge(qk_normed, g * 2 + 2)
                            for c in range(2):
                                k_c = kn[:, c * GC:(c + 1) * GC]
                                nc.tensor.matmul(ps[:, 4, c * GC:(c + 1) * GC], k_c, k_c, start=True, stop=True)
                                last = nc.tensor.matmul(ps[:, 4, (2 + c) * GC:(3 + c) * GC], k_c,
                                                        qn[:, c * GC:(c + 1) * GC], start=True, stop=True)
                            last.then_inc(gram_ready, 1)
                            pe.wait_ge(upper_ready, g * 2 + 2)
                            nc.tensor.matmul(ps[:, 5, 0:T], ones, upper_g[:].rearrange("p a b -> p (a b)"),
                                             start=True, stop=True)
                            nc.tensor.transpose(ps[:, 5, 2 * GC:3 * GC], kn[:, 0:GC], ident).then_inc(gc_ready, 1)
                        if j == 2:
                            pe.wait_ge(cmat_ready, g * LEVELS + 1)
                            pe.wait_ge(k_tail_ready, g + 1)
                            for c in range(2):
                                last = nc.tensor.transpose(ps[:, 5, c * GC:(c + 1) * GC], cmat[:, 0, c, :], ident)
                            last.then_inc(c0_turned, 1)
                        if j >= 3 and j % 2 == 1 and j <= 13:
                            s = (j - 1) // 2
                            pe.wait_ge(cmat_ready, g * LEVELS + (s + 1))
                            pe.wait_ge(inv_ready, g * LEVELS + s)
                            for c in range(2):
                                last = nc.tensor.matmul(ps[:, 5, c * GC:(c + 1) * GC], cmat[:, s, c, :],
                                                        inv[:, 2 + c, :], start=True, stop=True)
                            last.then_inc(t1_ready, 1)
                        if j >= 4 and j % 2 == 0 and j <= 14:
                            s = (j - 2) // 2
                            pe.wait_ge(t1_copied, g * 6 + s)
                            if s == 1:
                                pe.wait_ge(a_qk_ready, g + 1)
                            for c in range(2):
                                if s < 6:
                                    nc.tensor.matmul(ps[:, 4, c * GC:(c + 1) * GC], t1[:, c, :], inv[:, c, :],
                                                     start=True, stop=True)
                                last = nc.tensor.matmul(ps[:, 4, (2 + c) * GC:(3 + c) * GC], inv[:, c, :],
                                                        t1[:, c, :], start=True, stop=True)
                            last.then_inc(step_ready, 1)
                        if j == 15:
                            pe.wait_ge(inv_ready, g * LEVELS + LEVELS)
                            pe.wait_ge(rhs0_ready, g + 1)
                            nc.tensor.matmul(ps[:, 6, 0:DH], inv[:, 2, :], rhs0[:], start=True,
                                             stop=True).then_inc(v0_ready, 1)
                        if j == 16:
                            pe.wait_ge(v0_copied, g + 1)
                            nc.tensor.matmul(ps[:, 6, DH:2 * DH], k_tail[:], v_new[:, 0, :], start=True,
                                             stop=True).then_inc(state_ready, 1)
                            nc.tensor.matmul(ps[:, 4, 0:GC], v_new[:, 0, :], a_qk[:, 0, :], start=True, stop=True)
                        if j == 17:
                            pe.wait_ge(state_copied, g + 1)
                            nc.tensor.matmul(ps[:, 6, 2 * DH:3 * DH], kn[:, GC:], state[:], start=True,
                                             stop=True).then_inc(ks_ready, 1)
                        if j == 18:
                            pe.wait_ge(rhs1_steps, g * 2 + 2)
                            nc.tensor.matmul(ps[:, 6, 3 * DH:4 * DH], inv[:, 3, :], rhs1[:, 1, :], start=True,
                                             stop=True).then_inc(v1_ready, 1)
                        if j == 19:
                            pe.wait_ge(v1_copied, g + 1)
                            pe.wait_ge(qe_ready, g + 1)
                            nc.tensor.matmul(ps[:, 4, GC:2 * GC], state[:], qe[:], start=True, stop=False)
                            nc.tensor.matmul(ps[:, 4, GC:2 * GC], v_new[:, 1, :], a_qk[:, 1, :], start=False,
                                             stop=True).then_inc(o_ready, 1)
                        if j == 20:
                            pe.wait_ge(o_sq_ready, g + 1)
                            nc.tensor.matmul(ps[:, 5, 0:T], ones, o_sq[:], start=True, stop=True).then_inc(o_summed, 1)
                        if j == 5:
                            pe.wait_ge(scaled, g * HEAD_TILES + 7)
                            for c in range(2):
                                last = nc.tensor.transpose(ps[:, 7, c * GC:(c + 1) * GC],
                                                           att[:, 2, c * GC:(c + 1) * GC], ident)
                            last.then_inc(av_turned, 1)
                        if j == 6:
                            pe.wait_ge(att_sq_ready, g + 1)
                            pe.wait_ge(av_copied, g + 1)
                            nc.tensor.matmul(ps[:, 7, :], ones, att_sq[:].rearrange("p a b -> p (a b)"),
                                             start=True, stop=True).then_inc(att_summed, 1)
                        if j == 9:
                            pe.wait_ge(att_normed, g * 2 + 2)
                            nc.tensor.matmul(ps[:, 7, 0:GC], att_n[:, 0, 0:GC], att_n[:, 1, 0:GC], start=True, stop=True)
                            nc.tensor.matmul(ps[:, 7, GC:SCORES], att_n[:, 0, GC:], att_n[:, 1, :], start=True,
                                             stop=True).then_inc(score_ready, 1)
                        if j == 12:
                            pe.wait_ge(prob_ready, g * 2 + 2)
                            for c in range(3):
                                last = nc.tensor.transpose(ps[:, 7, c * GC:(c + 1) * GC], score[:, c * GC:(c + 1) * GC],
                                                           ident)
                            last.then_inc(prob_turned, 1)
                        if j == 13:
                            pe.wait_ge(prob_copied, g + 1)
                            nc.tensor.matmul(ps[:, 7, 0:T], av_tok[:, 0, :], prob_t[:, 0:T], start=True, stop=False)
                            nc.tensor.matmul(ps[:, 7, GC:T], av_tok[:, 1, :], prob_t[:, T:], start=False,
                                             stop=True).then_inc(att_o_ready, 1)
                    if j == 21 and not ghost:
                        pe.wait_ge(qk_sq_ready, n + 1)
                        if kind != "first":
                            pe.wait_ge(o_copied, n)
                        nc.tensor.matmul(ps[:, 4, :], ones, qk_sq[:].rearrange("p a b -> p (a b)"), start=True,
                                         stop=True).then_inc(qk_summed, 1)
                        for c in range(2):
                            last = nc.tensor.transpose(ps[:, 6, c * GC:(c + 1) * GC],
                                                       qkvz[:, p, 2, c * GC:(c + 1) * GC], ident)
                        last.then_inc(v_turned, 1)

            head_period(U_HEADS, 0, 0, 0, "first")
            with pe.Fori(0, 3) as i:
                head_period(i * 56 + U_HEADS, 28, i * 2 + 1, 1, "")
                head_period(i * 56 + U_HEADS, 56, i * 2 + 2, 0, "")
            head_period(U_HEADS + 168, 28, 7, 1, "")
            head_period(U_GHOST, 0, 8, 0, "ghost")

            with pe.Fori(0, (GATES - GHOST_GATES) // 4) as i:
                for j in range(16):
                    if j % 4 == 0:
                        pe.wait_ge(tile_free, i * 4 + (T_GHOST + GHOST_GATES + j // 4 - 2))
                    unit(i * 16 + U_GATES, j, 4 * (j % 4), KT, j // 4, from_x)

            def branch_body(ub, m0, first):
                for t in range(4):
                    pe.wait_ge(tile_free, m0 + (T_BRANCH + t - (1 if first and t == 1 else 2)))
                    for j in range(4):
                        src = ya if j < 2 else yb
                        unit(ub, 4 * t + j, 4 * (j % 2), HEADS, 2 * t + j // 2, lambda kt, src=src: src[:, kt, :])

            pe.wait_ge(ya_lo, HEADS)
            pe.wait_ge(yb_lo, HEADS)
            branch_body(U_BRANCH, 0, True)
            with pe.Fori(1, 4) as i:
                branch_body(i * 16 + U_BRANCH, i * 4, False)

            def out_body(ub, m0, first):
                for j in range(16):
                    if j % 4 == 0:
                        pe.wait_ge(tile_free, m0 + (T_OUT + j // 4 - 2))
                    if first and j < 4:
                        pe.wait_ge(mixed_lo, 4 * j + 4)
                    unit(ub, j, 4 * (j % 4), KT, j // 4, lambda kt: mixed[:, kt, :])

            out_body(U_OUT, 0, True)
            with pe.Fori(1, 4) as i:
                out_body(i * 16 + U_OUT, i * 4, False)

            gu_phase(2, U_GU2, T_GU2)
            down_phase(FT, U_DOWN2, T_DOWN2)

            pe.wait_ge(p_lo, 1)
            for j in range(8):
                pe.wait_ge(tile_free, T_PROJ + {0: -2, 1: 0}.get(j, j - 1))
                pe.wait_ge(lo_ready, U_PROJ + j + 1)
                for i in range(UK):
                    bank, kt = 2 * (j % 2) + i // 2, i % 2
                    hi, lo = (w[:, j % HL, i * P:(i + 1) * P] for w in (w_hi, w_lo))
                    if kt == 0:
                        nc.tensor.matmul(ps[:, bank, :], hi, p_hl[:, 0, :], start=True, stop=False)
                        nc.tensor.matmul(ps[:, bank, 0:T], lo, p_hl[:, 0, 0:T], start=False, stop=False)
                    else:
                        nc.tensor.matmul(ps[:, bank, 0:T], lo, p_hl[:, 1, 0:T], start=False, stop=False)
                        last = nc.tensor.matmul(ps[:, bank, :], hi, p_hl[:, 1, :], start=False, stop=True)
                last.then_inc(unit_used, 1)
                if j == 5:
                    norm_visit(3)

            def ple_body(ub, m0, first):
                for j in range(16):
                    if j % 4 == 0:
                        back = {0: 1, 4: 1}.get(j, 2) if first else 2
                        pe.wait_ge(tile_free, m0 + (T_PLE + j // 4 - back))
                    if first and j < 4:
                        pe.wait_ge(xw_lo, 3 * KT + 4 * j + 4)
                    unit(ub, j, 4 * (j % 4), KT, j // 4, from_x)

            ple_body(U_PLE, 0, True)
            with pe.Fori(1, 4) as i:
                ple_body(i * 16 + U_PLE, i * 4, False)


def weight_units(w):
    k, m = w.shape
    return w.reshape(k // UC, UK, P, m // P, P).transpose(3, 0, 2, 1, 4).reshape(m // P, k // UC, P, UC)


def pack_weights(i):
    ffn = []
    for name in ("ffn1", "ffn2"):
        gu = i[f"{name}_w_gu"][0]
        gate, up = weight_units(gu[:, :FF]), weight_units(gu[:, FF:])
        ffn.append([np.concatenate([gate, up], 1).reshape(-1, P, UC),
                    weight_units(i[f"{name}_w_down"][0]).reshape(-1, P, UC)])
    w_in, width = i["w_in"][0], HEADS * DH
    z = 3 * width
    att = z + width + 2 * HEADS
    gate = att + 3 * width
    tiles = [weight_units(w_in[:, o:o + width]) for o in
             (0, width, 2 * width, z, att, att + width, att + 2 * width)]
    heads = np.stack(tiles, 1).reshape(-1, P, UC)
    gates = np.stack([weight_units(w_in[:, gate:gate + D]), weight_units(w_in[:, gate + D:])], 1).reshape(-1, P, UC)
    branch = np.concatenate([weight_units(i["w_branch_a"][0]), weight_units(i["w_branch_b"][0])], 1).reshape(-1, P, UC)
    proj = i["ple_proj"][0].reshape(2, P, KT // 2, 2, P).transpose(2, 1, 3, 0, 4).reshape(-1, P, UC)
    units = np.concatenate([*ffn[0], heads, gates, branch, weight_units(i["w_out"][0]).reshape(-1, P, UC), *ffn[1],
                            proj, weight_units(i["ple_gate"][0]).reshape(-1, P, UC)])
    assert len(units) == UNITS
    return units.reshape(UNITS // 2, 2, P, UC).transpose(0, 2, 1, 3).reshape(UNITS // 2, P, 2 * UC)


def constants():
    a = np.arange(P)
    row, colm = a[:, None], a[None, :]
    parts = [np.eye(P), np.ones((P, P)), row <= colm]
    for s in range(LEVELS):
        parts.append((row >> (s + 1) == colm >> (s + 1)) & ((row >> s) & 1 == 1) & ((colm >> s) & 1 == 0))
    return np.stack(parts, 1).astype(np.float32)


def kernel(**inputs):
    import concourse.bacc as bacc
    from concourse.bass_utils import run_bass_kernel_spmd

    i = {k: np.asarray(v) for k, v in inputs.items()}

    def blocks(v):
        return np.swapaxes(v.reshape(-1, P, *v.shape[1:]), 0, 1)

    def rows(v):
        return np.broadcast_to(v, (P, v.size))

    conv = i["conv_w"][0].reshape(CONV_K, 3, HEADS, P).transpose(3, 2, 1, 0).reshape(P, -1)
    params = np.concatenate(
        [blocks(i[n][0]) for n in ("ffn1_norm", "mix_norm", "ffn2_norm", "ple_norm")] + [conv]
        + [i[n][0].reshape(P, 1) for n in ("gdn_norm", "q_norm", "k_norm")]
        + [rows(i["dt_bias"][0]), rows(i["a_log"][0])], 1)
    assert params.shape == (P, N_PARAM)
    w_in = i["w_in"][0]
    ab0 = 4 * HEADS * DH
    query = np.concatenate([np.tile(np.arange(P)[:, None], (1, GC)), np.tile(P + np.arange(P)[:, None], (1, T))], 1)
    key = np.concatenate([np.arange(GC), np.arange(T)])[None, :]
    rel = np.clip(query - key, -(CHUNK - 1), MAX_REL) + (CHUNK - 1)
    bias = np.where(key // CHUNK <= query // CHUNK, i["rel_bias"][0][:, rel], np.float32(NEG_INF))
    arrays = {
        "wstream": pack_weights(i),
        "x_t": blocks(i["x"][0].T),
        "p_t": blocks(i["p"][0, 0].T),
        "consts": constants(),
        "params": params,
        "w_ab": blocks(w_in[:, ab0:ab0 + 2 * HEADS]).reshape(P, -1),
        "rel_bias_rows": bias.transpose(1, 0, 2),
    }
    arrays = {k: np.ascontiguousarray(v) for k, v in arrays.items()}
    nc = bacc.Bacc("TRN2", target_bir_lowering=False, num_devices=1, dynamic_dma_scratch_size=1024)
    args = [nc.dram_tensor(k, v.shape, F32, kind="ExternalInput").ap() for k, v in arrays.items()]
    out = nc.dram_tensor("y_t", (4, P, 4, T), F32, kind="ExternalOutput").ap()
    build(nc, *args, out)
    got = run_bass_kernel_spmd(nc, [arrays], core_ids=[0]).results[0]["y_t"]
    return np.ascontiguousarray(got.transpose(0, 2, 1, 3).reshape(D, T).T)[None]
```

```python
from contextlib import ExitStack

import numpy as np

import concourse.bass as bass
from concourse import mybir

F32 = mybir.dt.float32
F32R = mybir.dt.float32r
ACT = mybir.ActivationFunctionType
ALU = mybir.AluOpType
AX = mybir.AxisListType

P = 128
T = 256
D = 2048
FF = 5632
PLE = 256
HEADS = 8
DH = 128
CONV_K = 4
CHUNK = 64
GC = 128
MAX_REL = 128
EPS = 1e-6
NEG_INF = -1e30

KT = D // P
FT = FF // P
UK = 4
UC = UK * P
RAW = 8
HL = 4
SQ = 4
ACT_SQ = 4
CHUNK_SLOTS = RAW // 2
LEVELS = 7

HEAD_TILES = 7
HEAD_UNITS = HEAD_TILES * KT // UK
GHOST_GATES = 8
GATES = 2 * KT

U_GU1 = 0
U_DOWN1 = U_GU1 + FT * 2 * KT // UK
U_HEADS = U_DOWN1 + KT * FT // UK
U_GHOST = U_HEADS + HEADS * HEAD_UNITS
U_GATES = U_GHOST + GHOST_GATES * KT // UK
U_BRANCH = U_GATES + (GATES - GHOST_GATES) * KT // UK
U_OUT = U_BRANCH + KT * 2 * HEADS // UK
U_GU2 = U_OUT + KT * KT // UK
U_DOWN2 = U_GU2 + FT * 2 * KT // UK
PROJ_UNITS = KT * (PLE // P) // UK
U_PLE = U_DOWN2 + KT * FT // UK + PROJ_UNITS
UNITS = U_PLE + KT * KT // UK

T_GU1 = 0
T_DOWN1 = T_GU1 + FT
T_HEADS = T_DOWN1 + KT
T_GHOST = T_HEADS + HEADS * HEAD_TILES
T_BRANCH = T_GHOST + GATES
T_OUT = T_BRANCH + KT
T_GU2 = T_OUT + KT
T_DOWN2 = T_GU2 + FT
T_PLE = T_DOWN2 + KT + PROJ_UNITS

C_IDENT, C_UPPER, C_MASKS = 0, 1, 2
N_CONST = C_MASKS + LEVELS
P_NORMS = 0
P_CONV = P_NORMS + 4 * KT
P_GDN_NORM = P_CONV + HEADS * 3 * CONV_K
P_Q_NORM = P_GDN_NORM + 1
P_K_NORM = P_Q_NORM + 1
P_DT = P_K_NORM + 1
P_ALOG = P_DT + HEADS
N_PARAM = P_ALOG + HEADS
FIRST_UNITS = [(j % 2, j // 2) for j in range(8)]
NORM_BANK = 7
BANK_OF_HEAD_TILE = [0, 1, 2, 3, 0, 1, 2]
K_G, K_GC, K_BETA, K_NEG_BETA, K_EXP_GC, K_TAIL, N_COL = 0, 2, 4, 6, 7, 8, 9
SCORES = GC + T


def down_unit(m, proj):
    return m * FT // UK + (m // 2 if proj else 0)


def down_tile(m, proj):
    return m + (m // 2 if proj else 0)


def build(nc, wstream, x_in, p_in, consts_in, params_in, wab_in, bias_in, y_out):
    ctx = ExitStack()
    with ctx:
        def sb(name, shape, dt=F32, stack=ctx):
            return stack.enter_context(nc.sbuf_tensor(name, shape, dt))

        def sem(name):
            return ctx.enter_context(nc.semaphore(name))

        raw = sb("raw", [P, RAW, UC])
        w_hi = sb("w_hi", [P, HL, UC], F32R)
        w_lo = sb("w_lo", [P, HL, UC], F32R)
        x = sb("x", [P, KT, T])
        xw = sb("xw", [P, KT, 2 * T], F32R)
        const = sb("const", [P, N_CONST, P])
        par = sb("par", [P, N_PARAM])
        eps = sb("eps", [P, 1])
        unread = sb("unread", [P, 1])
        r = sb("r", [P, T])
        r_ln = sb("r_ln", [P, T])
        ones = sb("ones", [P, P])
        xsq = sb("xsq", [P, SQ, T])
        acc = sb("acc", [P, T])
        part = sb("part", [P, 2, 2 * T])
        whole = sb("whole", [P, 2, 2 * T])
        act2 = sb("act2", [P, 2, T])
        prod = sb("prod", [P, 2, T])

        ffn = ExitStack()
        hid = sb("hid", [P, FT, 2 * T], F32R, ffn)
        ffn.close()
        mix = ExitStack()
        ya = sb("ya", [P, HEADS, 2 * T], F32R, mix)
        yb = sb("yb", [P, HEADS, 2 * T], F32R, mix)
        gdn = ExitStack()
        sb("first_gates", [P, GHOST_GATES, T], F32, gdn)

        def gs(name, shape):
            return sb(name, shape, F32, gdn)

        padded = gs("padded", [P, 3, CONV_K - 1 + T])
        taps = gs("taps", [P, 3 * CONV_K])
        tap = gs("tap", [P, T])
        conv = gs("conv", [P, 4, T])
        qkvz = gs("qkvz", [P, 2, 4, T])
        qk_sq = gs("qk_sq", [P, 2, T])
        qn = gs("qn", [P, T])
        kn = gs("kn", [P, T])
        qe = gs("qe", [P, GC])
        ab = gs("ab", [P, 2, 2 * HEADS])
        ab_part = gs("ab_part", [2 * HEADS, T])
        ab_row = gs("ab_row", [2 * HEADS, 2, T])
        t16 = gs("t16", [P, 8, 2 * HEADS])
        cols = gs("cols", [P, N_COL, HEADS])
        hcol = gs("hcol", [P, 2, N_COL])
        upper_g = gs("upper_g", [P, 2, GC])
        v_tok = gs("v_tok", [P, 2, DH])
        k_tail = gs("k_tail", [P, DH])
        decay = gs("decay", [P, 4, GC])
        exp_gc = gs("exp_gc", [P, GC])
        a_qk = gs("a_qk", [P, 2, GC])
        lmat = gs("lmat", [P, 2, GC])
        cmat = gs("cmat", [P, LEVELS, 2, GC])
        inv = gs("inv", [P, 4, GC])
        t1 = gs("t1", [P, 2, GC])
        rhs0 = gs("rhs0", [P, DH])
        rhs1 = gs("rhs1", [P, 2, DH])
        v_new = gs("v_new", [P, 2, DH])
        state = gs("state", [P, DH])
        o_sq = gs("o_sq", [P, T])
        y_gdn = gs("y_gdn", [P, 2, T])
        att = gs("att", [P, 3, T])
        att_sq = gs("att_sq", [P, 2, T])
        att_n = gs("att_n", [P, 2, T])
        av_tok = gs("av_tok", [P, 2, DH])
        score = gs("score", [P, SCORES])
        prob_t = gs("prob_t", [P, SCORES])
        smax = gs("smax", [P, 2])
        sneg = gs("sneg", [P, 2])
        ssum = gs("ssum", [P, 2])
        sinv = gs("sinv", [P, 2])
        wab = gs("wab", [P, KT * 2 * HEADS])
        wab_hi = sb("wab_hi", [P, KT * 2 * HEADS], F32R, gdn)
        wab_lo = sb("wab_lo", [P, KT * 2 * HEADS], F32R, gdn)
        bias = gs("bias", [P, HEADS, SCORES])
        gdn.close()
        gates = sb("gates", [P, GATES, T], F32, mix)
        mixed = sb("mixed", [P, KT, 2 * T], F32R, mix)
        sig = sb("sig", [P, 2, 2, T], F32, mix)
        mixed_f = sb("mixed_f", [P, 2, T], F32, mix)
        mix.close()
        ple = ExitStack()
        gate_s = sb("gate_s", [P, 2, T], F32, ple)
        y = sb("y", [P, KT, T], F32, ple)
        sb("behind_hidden", [P, FT * 2 * T - (KT + 2) * T], F32, ple)
        emb = sb("emb", [P, KT, T], F32, ple)
        p_raw = sb("p_raw", [P, PLE // P, T], F32, ple)
        p_hl = sb("p_hl", [P, PLE // P, 2 * T], F32R, ple)
        ple.close()

        ps = ctx.enter_context(nc.psum_tensor("ps", [P, 8, 2 * T], F32))
        ident, upper = const[:, C_IDENT, :], const[:, C_UPPER, :]

        def both(ap):
            return ap.unsqueeze(1).to_broadcast([P, 2, ap.shape[-1]])

        chunk_landed = [sem(f"chunk_landed{i}") for i in range(CHUNK_SLOTS)]
        x_landed = [sem(f"x_landed{i}") for i in range(4)]
        const_landed = sem("const_landed")
        par_landed = sem("par_landed")
        mix_landed = sem("mix_landed")
        p_landed = sem("p_landed")
        y_stored = sem("y_stored")
        hi_ready = sem("hi_ready")
        lo_ready = sem("lo_ready")
        unit_used = sem("unit_used")
        part_ready = sem("part_ready")
        tile_free = sem("tile_free")
        x_new = sem("x_new")
        xsq_ready = sem("xsq_ready")
        acc_added = sem("acc_added")
        xw_hi = sem("xw_hi")
        xw_lo = sem("xw_lo")
        norm_summed = sem("norm_summed")
        r_logged = sem("r_logged")
        r_ready = sem("r_ready")
        ones_set = sem("ones_set")
        gu_scaled = sem("gu_scaled")
        gu_silu = sem("gu_silu")
        hid_new = sem("hid_new")
        hid_hi = sem("hid_hi")
        hid_lo = sem("hid_lo")
        scaled = sem("scaled")
        pad_zero = sem("pad_zero")
        conv_steps = sem("conv_steps")
        taps_ready = sem("taps_ready")
        silu_done = sem("silu_done")
        qk_sq_ready = sem("qk_sq_ready")
        qk_summed = sem("qk_summed")
        v_turned = sem("v_turned")
        v_copied = sem("v_copied")
        qk_steps = sem("qk_steps")
        qk_normed = sem("qk_normed")
        wab_split = sem("wab_split")
        wab_lo_ready = sem("wab_lo_ready")
        ab_product = sem("ab_product")
        ab_copied = sem("ab_copied")
        ab_ready = sem("ab_ready")
        ab_steps = sem("ab_steps")
        ab_acts = sem("ab_acts")
        gc_summed = sem("gc_summed")
        hcol_ready = sem("hcol_ready")
        upper_ready = sem("upper_ready")
        gram_ready = sem("gram_ready")
        gc_ready = sem("gc_ready")
        arg_ready = sem("arg_ready")
        decay_ready = sem("decay_ready")
        exp_gc_ready = sem("exp_gc_ready")
        k_tail_ready = sem("k_tail_ready")
        lmat_ready = sem("lmat_ready")
        incl_ready = sem("incl_ready")
        cmat_ready = sem("cmat_ready")
        a_qk_ready = sem("a_qk_ready")
        qe_ready = sem("qe_ready")
        c0_turned = sem("c0_turned")
        inv_ready = sem("inv_ready")
        t1_ready = sem("t1_ready")
        t1_copied = sem("t1_copied")
        step_ready = sem("step_ready")
        rhs0_ready = sem("rhs0_ready")
        v0_ready = sem("v0_ready")
        v0_copied = sem("v0_copied")
        state_ready = sem("state_ready")
        state_copied = sem("state_copied")
        ks_ready = sem("ks_ready")
        rhs1_steps = sem("rhs1_steps")
        v1_ready = sem("v1_ready")
        v1_copied = sem("v1_copied")
        o_ready = sem("o_ready")
        o_sq_ready = sem("o_sq_ready")
        o_summed = sem("o_summed")
        o_steps = sem("o_steps")
        y_steps = sem("y_steps")
        first_sq = sem("first_sq")
        ya_hi = sem("ya_hi")
        ya_lo = sem("ya_lo")
        att_sq_ready = sem("att_sq_ready")
        av_turned = sem("av_turned")
        av_copied = sem("av_copied")
        att_summed = sem("att_summed")
        att_steps = sem("att_steps")
        att_normed = sem("att_normed")
        score_ready = sem("score_ready")
        score_steps = sem("score_steps")
        exp_done = sem("exp_done")
        sinv_ready = sem("sinv_ready")
        prob_ready = sem("prob_ready")
        prob_turned = sem("prob_turned")
        prob_copied = sem("prob_copied")
        att_o_ready = sem("att_o_ready")
        yb_hi = sem("yb_hi")
        yb_lo = sem("yb_lo")
        sig_ready = sem("sig_ready")
        branch_steps = sem("branch_steps")
        mixed_hi = sem("mixed_hi")
        mixed_lo = sem("mixed_lo")
        p_hi = sem("p_hi")
        p_lo = sem("p_lo")
        ple_scaled = sem("ple_scaled")
        ple_sig = sem("ple_sig")
        y_parts = sem("y_parts")

        block = ctx.enter_context(nc.Block())

        @block.sync
        def _(sp):
            for i in range(4):
                sp.dma_start(x[:, 4 * i:4 * i + 4, :], x_in[:, 4 * i:4 * i + 4, :]).then_inc(x_landed[i], 16)
                sp.dma_start(raw[:, 2 * i:2 * i + 2, :].rearrange("p a b -> p (a b)"),
                             wstream[i]).then_inc(chunk_landed[i], 16)

            def load_chunks(i):
                for s in range(CHUNK_SLOTS):
                    sp.wait_ge(lo_ready, i * RAW + 2 * s + 2 - RAW)
                    sp.dma_start(raw[:, 2 * s:2 * s + 2, :].rearrange("p a b -> p (a b)"),
                                 wstream[CHUNK_SLOTS * i + s]).then_inc(chunk_landed[s], 16)

            with sp.Fori(1, U_DOWN1 // RAW) as i:
                load_chunks(i)
            sp.dma_start(const[:], consts_in).then_inc(const_landed, 16)
            sp.dma_start(wab[:], wab_in).then_inc(mix_landed, 16)
            sp.dma_start(bias[:], bias_in).then_inc(mix_landed, 16)
            with sp.Fori(U_DOWN1 // RAW, U_DOWN2 // RAW) as i:
                load_chunks(i)
            sp.wait_ge(unit_used, U_GU2)
            sp.dma_start(p_raw[:], p_in).then_inc(p_landed, 16)
            with sp.Fori(U_DOWN2 // RAW, UNITS // RAW) as i:
                load_chunks(i)

        @block.scalar
        def _(act):
            def split_hi(ub, k):
                if k % 2 == 0:
                    act.wait_ge(chunk_landed[(k // 2) % CHUNK_SLOTS], ub * 2 + (16 * (k // RAW) + 16))
                if not (isinstance(ub, int) and ub + k < HL):
                    act.wait_ge(unit_used, ub + (k + 1 - HL))
                nc.scalar.activation(w_hi[:, k % HL, :], raw[:, k % RAW, :], ACT.Copy).then_inc(hi_ready, 1)

            def copy_part(tile, par_, used, bank, pair=False):
                act.wait_ge(unit_used, used)
                if not (isinstance(tile, int) and tile < 2):
                    act.wait_ge(tile_free, tile - 1)
                if pair:
                    nc.scalar.activation(part[:, par_, :].rearrange("p (a b) -> p a b", a=2),
                                         ps[:, bank:bank + 2, T:], ACT.Copy).then_inc(part_ready, 1)
                else:
                    nc.scalar.activation(part[:, par_, 0:T], ps[:, bank, T:], ACT.Copy).then_inc(part_ready, 1)

            def x_block(round_, m, s):
                act.wait_ge(x_new, m + (1 + KT * (round_ - 1)))
                act.wait_ge(acc_added, m + (KT * round_ + 1 - SQ))
                nc.scalar.activation(xsq[:, s, :], x[:, m, :], ACT.Square).then_inc(xsq_ready, 1)
                weigh_hi(round_, m)

            def weigh_hi(round_, m):
                nc.scalar.activation(xw[:, m, 0:T], x[:, m, :], ACT.Copy,
                                     scale=par[:, bass.ds(m + (P_NORMS + KT * round_), 1)]).then_inc(xw_hi, 1)

            def norm_factor(round_):
                act.wait_ge(norm_summed, round_ + 1)
                nc.scalar.activation(r_ln[:], ps[:, NORM_BANK, 0:T], ACT.Ln, bias=eps[:], scale=1.0 / D).then_inc(r_logged, 1)
                act.wait_ge(r_logged, round_ + 1)
                nc.scalar.activation(r[:], r_ln[:], ACT.Exp, scale=-0.5).then_inc(r_ready, 1)

            def gu_silu_step(n, p):
                act.wait_ge(gu_scaled, n + 1)
                nc.scalar.activation(act2[:, p, :], whole[:, p, 0:T], ACT.Silu).then_inc(gu_silu, 1)

            def gu_hi_step(n, f, p):
                act.wait_ge(hid_new, n + 1)
                nc.scalar.activation(hid[:, f, 0:T], prod[:, p, :], ACT.Copy).then_inc(hid_hi, 1)

            act.dma_start(par[:], params_in).then_inc(par_landed, 16)
            nc.scalar.preload_act_table_set("natural_log_exp_and_others")
            act.wait_ge(par_landed, 16)
            for m in range(KT):
                if m % 4 == 0:
                    act.wait_ge(x_landed[m // 4], 16)
                weigh_hi(0, m)
                if m % 4 == 3:
                    split_hi(0, m // 2 - 1)
                    split_hi(0, m // 2)
            for m in range(KT - ACT_SQ, KT):
                nc.scalar.activation(xsq[:, m % SQ, :], x[:, m, :], ACT.Square).then_inc(
                    xsq_ready, 1 if m > KT - ACT_SQ else m + 1)

            def gu_tile(ub, k0, n0, f, p, u0, t0, first, older):
                for j in range(8):
                    if j == 1 and older:
                        gu_hi_step(n0 + f - 2, f - 2, p)
                    if first and k0 + j == 14:
                        norm_factor(first - 1)
                    if j == 4 and (not first or k0 > 0):
                        copy_part(t0 + f - 1, (1 - p), u0 + 8 * f, 2 * (1 - p), pair=True)
                    if j == 7 and (not first or k0 > 0):
                        gu_silu_step(n0 + f - 1, 1 - p)
                    if n0 == FT and first and k0 == 0:
                        out_tail(j)
                    if not (first == 1 and k0 + j < 8):
                        split_hi(ub, k0 + j)

            def out_tail(j):
                m = 14 + j // 4
                if j % 4 == 0:
                    copy_part(T_OUT + m, m % 2, U_OUT + 4 * (m + 1), m % 4)
                if j % 4 == 2:
                    x_block(2, m, m % SQ)

            def gu_phase(round_, n0, u0, t0):
                gu_tile(u0, 0, n0, 0, 0, u0, t0, round_ + 1, False)
                gu_tile(u0, 8, n0, 1, 1, u0, t0, round_ + 1, False)
                with act.Fori(1, FT // 2) as i:
                    gu_tile(i * 16 + u0, 0, n0, i * 2, 0, u0, t0, 0, True)
                    gu_tile(i * 16 + u0, 8, n0, i * 2 + 1, 1, u0, t0, 0, True)

            def down_copy(m, u0, t0, proj):
                place = down_tile(m, proj)
                copy_part(t0 + place, place % 2, u0 + down_unit(m, proj) + FT // UK, m % 4)

            def proj_copy(b):
                place = 3 * b + 2
                copy_part(T_DOWN2 + place, place % 2, U_DOWN2 + down_unit(2 * b + 2, True), 4 + 2 * (b % 2), pair=True)

            def down_phase(round_, n0, u0, t0, gu_u, gu_t):
                proj = n0 > 0
                for m in range(KT):
                    for j in range(FT // UK):
                        if m == 0:
                            if j == 0 and proj:
                                act.wait_ge(p_landed, 16)
                                nc.scalar.activation(p_hl[:, :, 0:T], p_raw[:], ACT.Copy).then_inc(p_hi, 1)
                            if j == 1:
                                gu_hi_step(n0 + FT - 2, FT - 2, 0)
                            if j == 4:
                                copy_part(gu_t + FT - 1, 1, gu_u + 8 * FT, 2, pair=True)
                            if j == 7:
                                gu_silu_step(n0 + FT - 1, 1)
                            if j == 9:
                                gu_hi_step(n0 + FT - 1, FT - 1, 1)
                        else:
                            if j == 4:
                                down_copy(m - 1, u0, t0, proj)
                            if j == 6:
                                x_block(round_, m - 1, (m - 1) % SQ)
                            if j == 7 and proj and m % 2 == 0:
                                proj_copy(m // 2 - 1)
                        split_hi(u0, down_unit(m, proj) + j)
                    if proj and m % 2:
                        split_hi(u0, down_unit(m + 1, True) - 1)

            gu_phase(0, 0, U_GU1, T_GU1)
            down_phase(1, 0, U_DOWN1, T_DOWN1, U_GU1, T_GU1)

            def head_period(ub, k0, n, p, kind, tpar):
                g, q = n - 1, 1 - p
                tile0, unit0 = T_HEADS + HEAD_TILES * n, U_HEADS + HEAD_UNITS * n
                ghost = kind == "ghost"
                for j in range(32 if ghost else HEAD_UNITS):
                    if kind != "first":
                        if j == 4:
                            act.wait_ge(arg_ready, g * 4 + 2)
                            nc.scalar.activation(decay[:, 0:2, :], decay[:, 0:2, :], ACT.Exp,
                                                 scale=-1.0).then_inc(decay_ready, 1)
                            act.wait_ge(arg_ready, g * 4 + 4)
                            nc.scalar.activation(decay[:, 2:4, :], decay[:, 2:4, :], ACT.Exp).then_inc(decay_ready, 1)
                            nc.scalar.activation(exp_gc[:], ps[:, 5, GC:2 * GC], ACT.Exp).then_inc(exp_gc_ready, 1)
                            nc.scalar.activation(k_tail[:], ps[:, 5, 2 * GC:3 * GC], ACT.Copy,
                                                 scale=hcol[:, q, K_TAIL:K_TAIL + 1]).then_inc(k_tail_ready, 1)
                        if j >= 7 and j % 2 == 1 and j <= 17:
                            act.wait_ge(t1_ready, g * 6 + (j - 5) // 2)
                            nc.scalar.activation(t1[:].rearrange("p a b -> p (a b)"), ps[:, 5, 0:T],
                                                 ACT.Copy).then_inc(t1_copied, 1)
                        if j == 19:
                            act.wait_ge(v0_ready, g + 1)
                            nc.scalar.activation(v_new[:, 0, :], ps[:, 6, 0:DH], ACT.Copy).then_inc(v0_copied, 1)
                        if j == 20:
                            act.wait_ge(state_ready, g + 1)
                            nc.scalar.activation(state[:], ps[:, 6, DH:2 * DH], ACT.Copy).then_inc(state_copied, 1)
                        if j == 22:
                            act.wait_ge(v1_ready, g + 1)
                            nc.scalar.activation(v_new[:, 1, :], ps[:, 6, 3 * DH:4 * DH],
                                                 ACT.Copy).then_inc(v1_copied, 1)
                        if j == 23:
                            act.wait_ge(o_ready, g + 1)
                            nc.scalar.activation(o_sq[:], ps[:, 4, 0:T], ACT.Square).then_inc(o_sq_ready, 1)
                        if j == 24:
                            act.wait_ge(o_summed, g + 1)
                            nc.scalar.activation(o_sq[:], ps[:, 5, 0:T], ACT.Ln, bias=eps[:],
                                                 scale=1.0 / DH).then_inc(o_steps, 1)
                            act.wait_ge(o_steps, g * 2 + 1)
                            nc.scalar.activation(o_sq[:], o_sq[:], ACT.Exp, scale=-0.5).then_inc(o_steps, 1)
                        if j == 26:
                            act.wait_ge(y_steps, g * 2 + 2)
                            nc.scalar.activation(ya[:, g, 0:T], y_gdn[:, 1, :], ACT.Copy).then_inc(ya_hi, 1)
                        if j == 6:
                            act.wait_ge(scaled, g * HEAD_TILES + 6)
                            nc.scalar.activation(att_sq[:], att[:, 0:2, :], ACT.Square).then_inc(att_sq_ready, 1)
                        if j == 9:
                            act.wait_ge(av_turned, g + 1)
                            nc.scalar.activation(av_tok[:].rearrange("p a b -> p (a b)"), ps[:, 7, 0:T],
                                                 ACT.Copy).then_inc(av_copied, 1)
                        if j == 10:
                            act.wait_ge(att_summed, g + 1)
                            nc.scalar.activation(att_sq[:].rearrange("p a b -> p (a b)"), ps[:, 7, :], ACT.Ln,
                                                 bias=eps[:], scale=1.0 / DH).then_inc(att_steps, 1)
                            act.wait_ge(att_steps, g * 2 + 1)
                            nc.scalar.activation(att_sq[:], att_sq[:], ACT.Exp, scale=-0.5).then_inc(att_steps, 1)
                        if j == 14:
                            act.wait_ge(score_steps, g * 4 + 4)
                            nc.scalar.activation(score[:, 0:GC], score[:, 0:GC], ACT.Exp, bias=sneg[:, 0:1],
                                                 accum_out=ssum[:, 0:1]).then_inc(exp_done, 1)
                            nc.scalar.activation(score[:, GC:], score[:, GC:], ACT.Exp, bias=sneg[:, 1:2],
                                                 accum_out=ssum[:, 1:2]).then_inc(exp_done, 1)
                        if j == 16:
                            act.wait_ge(prob_turned, g + 1)
                            nc.scalar.activation(prob_t[:], ps[:, 7, 0:SCORES], ACT.Copy).then_inc(prob_copied, 1)
                        if j == 17:
                            act.wait_ge(att_o_ready, g + 1)
                            nc.scalar.activation(yb[:, g, 0:T], ps[:, 7, 0:T], ACT.Copy).then_inc(yb_hi, 1)
                    else:
                        if j == 0:
                            act.wait_ge(mix_landed, 32)
                            nc.scalar.activation(wab_hi[:], wab[:], ACT.Copy).then_inc(wab_split, 1)
                        if j == 4:
                            copy_part(T_DOWN1 + KT - 1, 1, U_HEADS, 3)
                        if j == 6:
                            x_block(1, KT - 1, (KT - 1) % SQ)
                        if j == 11:
                            norm_factor(1)
                            act.wait_ge(ab_product, 1)
                            nc.scalar.activation(ab_part[:], ps[0:2 * HEADS, 5, T:], ACT.Copy).then_inc(ab_copied, 1)
                        if j == 13:
                            nc.scalar.preload_act_table_set("natural_log_exp_and_others")
                            act.wait_ge(ab_steps, 6)
                            nc.scalar.activation(t16[:, 2, :], t16[:, 1, :], ACT.Exp, scale=-1.0).then_inc(ab_acts, 1)
                            act.wait_ge(ab_acts, 1)
                            nc.scalar.activation(t16[:, 3, :], t16[:, 2, :], ACT.Ln,
                                                 bias=ones[:, 0:1]).then_inc(ab_acts, 1)
                            nc.scalar.activation(t16[:, 4, 0:HEADS], par[:, P_ALOG:P_ALOG + HEADS],
                                                 ACT.Exp).then_inc(ab_acts, 1)
                            nc.scalar.activation(cols[:, K_BETA:K_BETA + 2, :], ab[:, :, HEADS:],
                                                 ACT.Sigmoid).then_inc(ab_acts, 1)
                        if j == 20:
                            act.wait_ge(ab_steps, 11)
                            nc.scalar.activation(cols[:, K_EXP_GC, :], cols[:, K_GC + 1, :], ACT.Exp).then_inc(ab_acts, 1)
                            nc.scalar.activation(cols[:, K_TAIL, :], t16[:, 7, 0:HEADS], ACT.Exp).then_inc(ab_acts, 1)
                    if kind == "first" and j in (10, 12):
                        t = j // 2 - 5
                        copy_part(tile0 + t, t, unit0 + 7 + t, BANK_OF_HEAD_TILE[t])
                    if j % 4 == 0 and not (kind == "first" and j <= 12):
                        t = j // 4 - 2
                        if t >= 0:
                            bank = t % 4 if ghost else BANK_OF_HEAD_TILE[t]
                            copy_part(tile0 + t, (tpar + t) % 2, unit0 + 4 * (t + 1), bank)
                        else:
                            copy_part(tile0 + t, (tpar + t) % 2, unit0 + 4 * (t + 1),
                                      BANK_OF_HEAD_TILE[HEAD_TILES + t])
                    if j == (23 if kind == "first" else 21) and not ghost:
                        act.wait_ge(conv_steps, n * (6 * CONV_K) + 6 * CONV_K)
                        nc.scalar.activation(qkvz[:, p, 0:3, :], conv[:, 0:3, :], ACT.Silu).then_inc(silu_done, 1)
                        act.wait_ge(silu_done, n * 2 + 1)
                        nc.scalar.activation(qk_sq[:], qkvz[:, p, 0:2, :], ACT.Square).then_inc(qk_sq_ready, 1)
                    if j == 23 and not ghost:
                        act.wait_ge(scaled, n * HEAD_TILES + 4)
                        nc.scalar.activation(qkvz[:, p, 3, :], conv[:, 3, :], ACT.Silu).then_inc(silu_done, 1)
                        nc.scalar.preload_act_table_set("natural_log_exp_and_others")
                    if j == 26 and not ghost:
                        act.wait_ge(qk_summed, n + 1)
                        nc.scalar.activation(qk_sq[:].rearrange("p a b -> p (a b)"), ps[:, 7, :], ACT.Ln,
                                             bias=eps[:]).then_inc(qk_steps, 1)
                        act.wait_ge(qk_steps, n * 2 + 1)
                        nc.scalar.activation(qk_sq[:], qk_sq[:], ACT.Exp, scale=-0.5).then_inc(qk_steps, 1)
                    split_hi(ub, k0 + j)
                    if j == (20 if kind == "first" else 18) and not ghost:
                        nc.scalar.preload_act_table_set("silu_and_others")

            head_period(U_HEADS, 0, 0, 0, "first", 0)
            with act.Fori(0, 3) as i:
                head_period(i * 56 + U_HEADS, 28, i * 2 + 1, 1, "", 1)
                head_period(i * 56 + U_HEADS, 56, i * 2 + 2, 0, "", 0)
            head_period(U_HEADS + 168, 28, 7, 1, "", 1)
            head_period(U_GHOST, 0, 8, 0, "ghost", 0)

            def gates_body(ub, tile0, unit0):
                for j in range(16):
                    if j % 4 == 0:
                        t = j // 4 - 2
                        copy_part(tile0 + t, t % 2, unit0 + 4 * (t + 1), t % 4)
                    split_hi(ub, j)

            with act.Fori(0, (GATES - GHOST_GATES) // 4) as i:
                gates_body(i * 16 + U_GATES, i * 4 + (T_GHOST + GHOST_GATES), i * 16 + U_GATES)

            def branch_tile(m, m4):
                copy_part(m + T_BRANCH, m4 % 2, m * 4 + (U_BRANCH + 4), 2 * m4, pair=True)
                if not (isinstance(m, int) and m < 2):
                    act.wait_ge(branch_steps, m * 2 - 2)
                else:
                    act.wait_ge(scaled, HEADS * HEAD_TILES + GATES)
                nc.scalar.activation(sig[:, m4 % 2], gates[:, bass.ds(m * 2, 2), :], ACT.Sigmoid).then_inc(sig_ready, 1)

            def branch_hi(m, s):
                act.wait_ge(branch_steps, m * 2 + 2)
                nc.scalar.activation(mixed[:, m, 0:T], mixed_f[:, s, :], ACT.Copy).then_inc(mixed_hi, 1)

            def branch_body(ub, m0, first):
                for j in range(16):
                    t = j // 4 - 2
                    if j % 4 == 0:
                        if first and t < 0:
                            tile = T_BRANCH + t
                            copy_part(tile, t % 2, U_BRANCH + 4 * (t + 1), t % 4)
                        else:
                            branch_tile(m0 + t, t % 4)
                    if j % 4 == 2 and not (first and t < 1):
                        branch_hi(m0 + (t - 1), (t - 1) % 2)
                    split_hi(ub, j)

            branch_body(U_BRANCH, 0, True)
            with act.Fori(1, 4) as i:
                branch_body(i * 16 + U_BRANCH, i * 4, False)

            def out_body(ub, m0, first):
                for j in range(16):
                    t = j // 4 - 2
                    if first and t < 0:
                        if j % 4 == 0:
                            branch_tile(KT + t, t % 4)
                        if j in (2, 6, 7):
                            b = {2: 13, 6: 14, 7: 15}[j]
                            branch_hi(b, b % 2)
                    elif first:
                        if j in (12, 14):
                            x_block(2, j // 2 - 6, j // 2 - 6)
                        if j in (10, 12):
                            copy_part(T_OUT + (j // 2 - 5), j // 2 - 5, U_OUT + (j // 2 + 2), j // 2 - 5)
                    else:
                        if j % 4 == 0:
                            copy_part(m0 + (T_OUT + t), t % 2, m0 * 4 + (U_OUT + 4 * (t + 1)), t % 4)
                        if j % 4 == 2:
                            x_block(2, m0 + t, t % SQ)
                    split_hi(ub, j)

            out_body(U_OUT, 0, True)
            with act.Fori(1, 4) as i:
                out_body(i * 16 + U_OUT, i * 4, False)

            gu_phase(2, FT, U_GU2, T_GU2)
            down_phase(3, FT, U_DOWN2, T_DOWN2, U_GU2, T_GU2)

            def ple_sig_step(m, s):
                act.wait_ge(ple_scaled, m + 1)
                nc.scalar.activation(act2[:, s, :], gate_s[:, s, :], ACT.Sigmoid).then_inc(ple_sig, 1)

            def store(i):
                act.wait_ge(y_parts, i * 8 + 8)
                act.dma_start(y_out[i], y[:, bass.ds(i * 4, 4), :]).then_inc(y_stored, 16)

            def store_last(m, n):
                act.wait_ge(y_parts, 2 * (m + n))
                act.dma_start(y_out[3, :, m - 12:m - 12 + n, :], y[:, m:m + n, :]).then_inc(y_stored, 16)

            def ple_body(ub, i, first):
                for j in range(16):
                    t = j // 4 - 2
                    if first:
                        if j == 4:
                            down_copy(KT - 1, U_DOWN2, T_DOWN2, True)
                        if j == 6:
                            x_block(3, KT - 1, (KT - 1) % SQ)
                        if j == 7:
                            proj_copy(PROJ_UNITS - 1)
                        if j == 11:
                            norm_factor(3)
                        if j in (10, 12):
                            copy_part(T_PLE + (j // 2 - 5), j // 2 - 5, U_PLE + (j // 2 + 2), j // 2 - 5)
                        if j in (14, 15):
                            ple_sig_step(j - 14, j - 14)
                    else:
                        if j % 4 == 0:
                            copy_part(i * 4 + (T_PLE + t), t % 2, i * 16 + (U_PLE + 4 * (t + 1)), t % 4)
                        if j % 4 == 3:
                            ple_sig_step(i * 4 + t, t % 2)
                        if j == 14:
                            store(i - 1)
                    split_hi(ub, j)

            ple_body(U_PLE, 0, True)
            with act.Fori(1, 4) as i:
                ple_body(i * 16 + U_PLE, i, False)
            for m in (14, 15):
                copy_part(T_PLE + m, m % 2, U_PLE + 4 * (m + 1), m % 4)
                ple_sig_step(m, m % 2)
                if m == KT - 1:
                    store_last(KT - 4, 3)
            store_last(KT - 1, 1)
            act.wait_ge(y_stored, 16 * 5)

        @block.vector
        def _(dve):
            def split_lo(ub, k):
                dve.wait_ge(hi_ready, ub + (k + 1))
                nc.vector.tensor_tensor(w_lo[:, k % HL, :], raw[:, k % RAW, :], w_hi[:, k % HL, :].bitcast(F32),
                                        ALU.subtract).then_inc(lo_ready, 1)

            def add_parts(tile, par_, bank, out=None, pair=False):
                dve.wait_ge(part_ready, tile + 1)
                if pair:
                    if out is None:
                        out = whole[:, par_, :].rearrange("p (a b) -> p a b", a=2)
                    nc.vector.tensor_tensor(out, ps[:, bank:bank + 2, 0:T],
                                            part[:, par_, :].rearrange("p (a b) -> p a b", a=2),
                                            ALU.add).then_inc(tile_free, 1)
                else:
                    nc.vector.tensor_tensor(whole[:, par_, 0:T], ps[:, bank, 0:T], part[:, par_, 0:T],
                                            ALU.add).then_inc(tile_free, 1)

            def x_update(round_, tile, m, par_, bank, half):
                add_parts(tile, par_, bank)
                dve.wait_ge(tile_free, tile + 1)
                if half:
                    ins = nc.vector.scalar_tensor_tensor(out=x[:, m, :], in0=whole[:, par_, 0:T], scalar=0.5,
                                                         in1=x[:, m, :], op0=ALU.mult, op1=ALU.add)
                else:
                    ins = nc.vector.tensor_tensor(x[:, m, :], whole[:, par_, 0:T], x[:, m, :], ALU.add)
                ins.then_inc(x_new, 1)

            def acc_add(round_, m, s):
                weigh_lo(round_, m)
                acc_square(round_, m, s)

            def weigh_lo(round_, m):
                dve.wait_ge(xw_hi, m + (KT * round_ + 1))
                nc.vector.scalar_tensor_tensor(out=xw[:, m, T:], in0=x[:, m, :],
                                               scalar=par[:, bass.ds(m + (P_NORMS + KT * round_), 1)],
                                               in1=xw[:, m, 0:T].bitcast(F32), op0=ALU.mult,
                                               op1=ALU.subtract).then_inc(xw_lo, 1)

            def acc_square(round_, m, s):
                dve.wait_ge(xsq_ready, m + (KT * round_ + 1))
                if isinstance(m, int) and m == (0 if round_ else KT - ACT_SQ):
                    if round_ > 0:
                        dve.wait_ge(norm_summed, round_)
                    nc.vector.tensor_copy(acc[:], xsq[:, s, :]).then_inc(acc_added, 1 if round_ else m + 1)
                else:
                    dve.wait_ge(acc_added, m + KT * round_)
                    nc.vector.tensor_tensor(acc[:], acc[:], xsq[:, s, :], ALU.add).then_inc(acc_added, 1)

            dve.wait_ge(par_landed, 16)
            nc.vector.memset(eps[:], EPS)
            nc.vector.memset(ones[:], 1.0).then_inc(ones_set, 1)
            for m in range(KT):
                weigh_lo(0, m)
                if m % 4 == 3:
                    split_lo(0, m // 2 - 1)
                    split_lo(0, m // 2)

            def gu_scale(tile, p):
                dve.wait_ge(tile_free, tile + 1)
                w2 = whole[:, p, :].rearrange("p (a b) -> p a b", a=2)
                nc.vector.tensor_tensor(w2, w2, both(r[:]), ALU.mult).then_inc(gu_scaled, 1)

            def gu_product(n, p):
                dve.wait_ge(gu_silu, n + 1)
                dve.wait_ge(hid_lo, n + 1)
                nc.vector.tensor_tensor(prod[:, p, :], act2[:, p, :], whole[:, p, T:], ALU.mult).then_inc(hid_new, 1)

            def out_tail(j):
                m = 14 + j // 4
                if j % 4 == 1:
                    x_update(2, T_OUT + m, m, m % 2, m % 4, False)
                if j % 4 == 3:
                    acc_add(2, m, m % SQ)

            def gu_tile(ub, k0, n0, f, p, t0, first, older):
                for j in range(8):
                    if j == 0 and older:
                        gu_product(n0 + f - 2, p)
                    if n0 == FT and first and k0 == 0:
                        out_tail(j)
                    if j == 5 and (not first or k0 > 0):
                        add_parts(t0 + f - 1, 1 - p, 2 * (1 - p), pair=True)
                        if not first:
                            gu_scale(t0 + f - 1, 1 - p)
                    if j == 6 and first and k0 > 0:
                        dve.wait_ge(r_ready, first)
                        gu_scale(t0 + f - 1, 1 - p)
                    if first == 1 and j < ACT_SQ and k0 > 0:
                        acc_square(0, KT - ACT_SQ + j, (KT - ACT_SQ + j) % SQ)
                    if not (first == 1 and k0 + j < 8):
                        split_lo(ub, k0 + j)

            def gu_phase(round_, n0, u0, t0):
                gu_tile(u0, 0, n0, 0, 0, t0, round_ + 1, False)
                gu_tile(u0, 8, n0, 1, 1, t0, round_ + 1, False)
                with dve.Fori(1, FT // 2) as i:
                    gu_tile(i * 16 + u0, 0, n0, i * 2, 0, t0, 0, True)
                    gu_tile(i * 16 + u0, 8, n0, i * 2 + 1, 1, t0, 0, True)

            def down_update(round_, m, t0, proj):
                place = down_tile(m, proj)
                x_update(round_, t0 + place, m, place % 2, m % 4, True)

            def proj_add(b):
                place = 3 * b + 2
                add_parts(T_DOWN2 + place, place % 2, 4 + 2 * (b % 2), emb[:, 2 * b:2 * b + 2, :], pair=True)

            def down_phase(round_, n0, u0, t0, gu_t):
                proj = n0 > 0
                for m in range(KT):
                    for j in range(FT // UK):
                        if m == 0:
                            if j == 0:
                                gu_product(n0 + FT - 2, 0)
                            if j == 1 and proj:
                                dve.wait_ge(p_hi, 1)
                                nc.vector.tensor_tensor(p_hl[:, :, T:], p_raw[:], p_hl[:, :, 0:T].bitcast(F32),
                                                        ALU.subtract).then_inc(p_lo, 1)
                            if j == 5:
                                add_parts(gu_t + FT - 1, 1, 2, pair=True)
                                gu_scale(gu_t + FT - 1, 1)
                            if j == 8:
                                gu_product(n0 + FT - 1, 1)
                        else:
                            if j == 5:
                                down_update(round_, m - 1, t0, proj)
                            if j == 7:
                                acc_add(round_, m - 1, (m - 1) % SQ)
                            if j == 8 and proj and m % 2 == 0:
                                proj_add(m // 2 - 1)
                        split_lo(u0, down_unit(m, proj) + j)
                    if proj and m % 2:
                        split_lo(u0, down_unit(m + 1, True) - 1)

            gu_phase(0, 0, U_GU1, T_GU1)
            down_phase(1, 0, U_DOWN1, T_DOWN1, T_GU1)

            def head_period(ub, k0, n, p, kind, tpar):
                g, q = n - 1, 1 - p
                tile0 = T_HEADS + HEAD_TILES * n
                ghost = kind == "ghost"
                col = lambda i: hcol[:, q, i:i + 1]
                for j in range(32 if ghost else HEAD_UNITS):
                    if kind != "first":
                        if j == 4:
                            dve.wait_ge(gc_ready, g + 1)
                            for c in range(2):
                                nc.vector.tensor_scalar(decay[:, c, :], ps[:, 5, c * GC:(c + 1) * GC], col(K_GC + c),
                                                        0.0, ALU.subtract, ALU.max).then_inc(arg_ready, 1)
                            for c in range(2):
                                nc.vector.tensor_scalar(decay[:, 2 + c, :], ps[:, 5, c * GC:(c + 1) * GC], col(K_GC + c),
                                                        0.0, ALU.subtract, ALU.min).then_inc(arg_ready, 1)
                            dve.wait_ge(decay_ready, g * 2 + 1)
                            dve.wait_ge(gram_ready, g + 1)
                            for c in range(2):
                                nc.vector.scalar_tensor_tensor(
                                    out=lmat[:, c, :], in0=ps[:, 4, c * GC:(c + 1) * GC], scalar=col(K_BETA + c),
                                    in1=decay[:, c, :], op0=ALU.mult, op1=ALU.mult).then_inc(lmat_ready, 1)
                        if j == 9:
                            nc.vector.tensor_scalar(rhs0[:], v_tok[:, 0, :], col(K_BETA), None,
                                                    ALU.mult).then_inc(rhs0_ready, 1)
                            dve.wait_ge(exp_gc_ready, g + 1)
                            nc.vector.tensor_tensor(qe[:], qn[:, GC:], exp_gc[:], ALU.mult).then_inc(qe_ready, 1)
                        if j == 6:
                            dve.wait_ge(incl_ready, g + 1)
                            nc.vector.tensor_tensor(a_qk[:].rearrange("p a b -> p (a b)"), ps[:, 4, 2 * GC:],
                                                    decay[:, 2:4, :].rearrange("p a b -> p (a b)"),
                                                    ALU.mult).then_inc(a_qk_ready, 1)
                        if j >= 8 and j % 2 == 0 and j <= 18:
                            s = (j - 6) // 2
                            dve.wait_ge(step_ready, g * 6 + s)
                            dve.wait_ge(inv_ready, g * LEVELS + s)
                            lo = 0 if s < 6 else 2
                            nc.vector.tensor_tensor(inv[:, lo:4, :].rearrange("p a b -> p (a b)"),
                                                    inv[:, lo:4, :].rearrange("p a b -> p (a b)"),
                                                    ps[:, 4, lo * GC:], ALU.subtract).then_inc(inv_ready, 1)
                        if j == 21:
                            dve.wait_ge(ks_ready, g + 1)
                            nc.vector.scalar_tensor_tensor(out=rhs1[:, 0, :], in0=ps[:, 6, 2 * DH:3 * DH],
                                                           scalar=col(K_EXP_GC), in1=v_tok[:, 1, :], op0=ALU.mult,
                                                           op1=ALU.subtract).then_inc(rhs1_steps, 1)
                            dve.wait_ge(rhs1_steps, g * 2 + 1)
                            nc.vector.tensor_scalar(rhs1[:, 1, :], rhs1[:, 0, :], col(K_NEG_BETA), None,
                                                    ALU.mult).then_inc(rhs1_steps, 1)
                        if j == 25:
                            dve.wait_ge(o_steps, g * 2 + 2)
                            nc.vector.scalar_tensor_tensor(out=y_gdn[:, 0, :], in0=ps[:, 4, 0:T],
                                                           scalar=par[:, P_GDN_NORM:P_GDN_NORM + 1], in1=o_sq[:],
                                                           op0=ALU.mult, op1=ALU.mult).then_inc(y_steps, 1)
                            dve.wait_ge(y_steps, g * 2 + 1)
                            dve.wait_ge(scaled, g * HEAD_TILES + 6)
                            nc.vector.tensor_tensor(y_gdn[:, 1, :], y_gdn[:, 0, :], qkvz[:, q, 3, :],
                                                    ALU.mult).then_inc(y_steps, 1)
                        if j == 11:
                            dve.wait_ge(att_steps, g * 2 + 2)
                            for i in range(2):
                                nc.vector.scalar_tensor_tensor(
                                    out=att_n[:, i, :], in0=att[:, i, :], scalar=par[:, P_Q_NORM + i:P_Q_NORM + i + 1],
                                    in1=att_sq[:, i, :], op0=ALU.mult, op1=ALU.mult).then_inc(att_normed, 1)
                        if j == 13:
                            dve.wait_ge(score_ready, g + 1)
                            nc.vector.scalar_tensor_tensor(out=score[:], in0=ps[:, 7, 0:SCORES], scalar=DH ** -0.5,
                                                           in1=bias[:, g, :], op0=ALU.mult,
                                                           op1=ALU.add).then_inc(score_steps, 1)
                            dve.wait_ge(score_steps, g * 4 + 1)
                            nc.vector.tensor_reduce(smax[:, 0:1], score[:, 0:GC], AX.X, ALU.max).then_inc(score_steps, 1)
                            nc.vector.tensor_reduce(smax[:, 1:2], score[:, GC:], AX.X, ALU.max).then_inc(score_steps, 1)
                            dve.wait_ge(score_steps, g * 4 + 3)
                            nc.vector.tensor_scalar(sneg[:], smax[:], -1.0, None, ALU.mult).then_inc(score_steps, 1)
                        if j == 15:
                            dve.wait_ge(exp_done, g * 2 + 2)
                            nc.vector.reciprocal(sinv[:], ssum[:]).then_inc(sinv_ready, 1)
                            dve.wait_ge(sinv_ready, g + 1)
                            nc.vector.tensor_scalar(score[:, 0:GC], score[:, 0:GC], sinv[:, 0:1], None,
                                                    ALU.mult).then_inc(prob_ready, 1)
                            nc.vector.tensor_scalar(score[:, GC:], score[:, GC:], sinv[:, 1:2], None,
                                                    ALU.mult).then_inc(prob_ready, 1)
                        if j == 18:
                            dve.wait_ge(yb_hi, g + 1)
                            nc.vector.tensor_tensor(yb[:, g, T:], ps[:, 7, 0:T], yb[:, g, 0:T].bitcast(F32),
                                                    ALU.subtract).then_inc(yb_lo, 1)
                    else:
                        if j == 0:
                            dve.wait_ge(wab_split, 1)
                            nc.vector.tensor_tensor(wab_lo[:], wab[:], wab_hi[:].bitcast(F32),
                                                    ALU.subtract).then_inc(wab_lo_ready, 1)
                        if j == 5:
                            x_update(1, T_DOWN1 + KT - 1, KT - 1, 1, 3, True)
                        if j == 7:
                            acc_add(1, KT - 1, (KT - 1) % SQ)
                        if j == 11:
                            dve.wait_ge(ab_copied, 1)
                            nc.vector.tensor_tensor(ab_row[:, 0, :], ps[0:2 * HEADS, 5, 0:T], ab_part[:],
                                                    ALU.add).then_inc(ab_steps, 1)
                            dve.wait_ge(ab_steps, 1)
                            dve.wait_ge(r_ready, 2)
                            nc.vector.tensor_tensor(ab_row[:, 1, :], ab_row[:, 0, :], r[0:2 * HEADS, :],
                                                    ALU.mult).then_inc(ab_steps, 1)
                        if j == 12:
                            dve.wait_ge(ab_ready, 1)
                            nc.vector.tensor_copy(ab[:].rearrange("p a b -> p (a b)"),
                                                  ps[:, 6, 0:4 * HEADS]).then_inc(ab_steps, 1)
                            dve.wait_ge(ab_steps, 3)
                            a_dt = t16[:, 0, :].rearrange("p (a b) -> p a b", a=2)
                            nc.vector.tensor_tensor(a_dt, ab[:, :, 0:HEADS], both(par[:, P_DT:P_DT + HEADS]),
                                                    ALU.add).then_inc(ab_steps, 1)
                            dve.wait_ge(ab_steps, 4)
                            nc.vector.tensor_scalar(t16[:, 5, :], t16[:, 0, :], -1.0, None, ALU.mult).then_inc(ab_steps, 1)
                            dve.wait_ge(ab_steps, 5)
                            nc.vector.tensor_tensor(t16[:, 1, :], t16[:, 0, :], t16[:, 5, :], ALU.max).then_inc(ab_steps, 1)
                        if j == 14:
                            dve.wait_ge(ab_acts, 4)
                            nc.vector.scalar_tensor_tensor(out=t16[:, 6, :], in0=t16[:, 0, :], scalar=0.0,
                                                           in1=t16[:, 3, :], op0=ALU.max,
                                                           op1=ALU.add).then_inc(ab_steps, 1)
                            dve.wait_ge(ab_steps, 7)
                            nc.vector.scalar_tensor_tensor(
                                out=cols[:, K_G:K_G + 2, :], in0=t16[:, 6, :].rearrange("p (a b) -> p a b", a=2),
                                scalar=-1.0, in1=both(t16[:, 4, 0:HEADS]), op0=ALU.mult,
                                op1=ALU.mult).then_inc(ab_steps, 1)
                            nc.vector.tensor_scalar(cols[:, K_NEG_BETA, :], cols[:, K_BETA + 1, :], -1.0, None,
                                                    ALU.mult).then_inc(ab_steps, 1)
                        if j == 19:
                            dve.wait_ge(gc_summed, 1)
                            nc.vector.tensor_copy(cols[:, K_GC:K_GC + 2, :],
                                                  ps[:, 5, 64:80].rearrange("p (a b) -> p a b", a=2)
                                                  ).then_inc(ab_steps, 1)
                            dve.wait_ge(ab_steps, 10)
                            nc.vector.tensor_tensor(t16[:, 7, 0:HEADS], ps[:, 5, 80:88], cols[:, K_GC, :],
                                                    ALU.subtract).then_inc(ab_steps, 1)
                    if kind == "first" and j in (11, 13):
                        t = j // 2 - 5
                        add_parts(tile0 + t, t, BANK_OF_HEAD_TILE[t])
                    if j % 4 == 1 and not (kind == "first" and j <= 13):
                        t = j // 4 - 2
                        if t >= 0:
                            bank = t % 4 if ghost else BANK_OF_HEAD_TILE[t]
                        else:
                            bank = BANK_OF_HEAD_TILE[HEAD_TILES + t]
                        dve.wait_ge(scaled, n * HEAD_TILES + (t - 1))
                        add_parts(tile0 + t, (tpar + t) % 2, bank)
                    if j == 26 and not ghost:
                        dve.wait_ge(v_turned, n + 1)
                        nc.vector.tensor_copy(v_tok[:].rearrange("p a b -> p (a b)"), ps[:, 6, 0:T]).then_inc(v_copied, 1)
                        dve.wait_ge(qk_steps, n * 2 + 2)
                        nc.vector.tensor_tensor(kn[:], qkvz[:, p, 1, :], qk_sq[:, 1, :], ALU.mult).then_inc(qk_normed, 1)
                        nc.vector.scalar_tensor_tensor(out=qn[:], in0=qkvz[:, p, 0, :], scalar=DH ** -0.5,
                                                       in1=qk_sq[:, 0, :], op0=ALU.mult,
                                                       op1=ALU.mult).then_inc(qk_normed, 1)
                    if j == 27 and not ghost:
                        if kind == "first":
                            dve.wait_ge(ab_acts, 6)
                            dve.wait_ge(const_landed, 16)
                        nc.vector.tensor_copy(hcol[:, p, :], cols[:, :, n]).then_inc(hcol_ready, 1)
                        dve.wait_ge(hcol_ready, n + 1)
                        for c in range(2):
                            nc.vector.tensor_scalar(upper_g[:, c, :], upper, hcol[:, p, K_G + c:K_G + c + 1], None,
                                                    ALU.mult).then_inc(upper_ready, 1)
                    if j == 5 and kind != "first":
                        dve.wait_ge(c0_turned, g + 1)
                        nc.vector.tensor_tensor(inv[:, 2:4, :], both(ident),
                                                ps[:, 6, 0:T].rearrange("p (a b) -> p a b", a=2), ALU.subtract)
                        nc.vector.tensor_tensor(inv[:, 0:2, :], both(ident), cmat[:, 0],
                                                ALU.subtract).then_inc(inv_ready, 1)
                    split_lo(ub, k0 + j)

            head_period(U_HEADS, 0, 0, 0, "first", 0)
            with dve.Fori(0, 3) as i:
                head_period(i * 56 + U_HEADS, 28, i * 2 + 1, 1, "", 1)
                head_period(i * 56 + U_HEADS, 56, i * 2 + 2, 0, "", 0)
            head_period(U_HEADS + 168, 28, 7, 1, "", 1)
            head_period(U_GHOST, 0, 8, 0, "ghost", 0)

            with dve.Fori(0, (GATES - GHOST_GATES) // 4) as i:
                for j in range(16):
                    if j % 4 == 1:
                        t = j // 4 - 2
                        dve.wait_ge(scaled, i * 4 + (HEADS * HEAD_TILES + GHOST_GATES + t - 1))
                        add_parts(i * 4 + (T_GHOST + GHOST_GATES + t), t % 2, t % 4)
                    split_lo(i * 16 + U_GATES, j)

            def branch_add(m, m4):
                if not (isinstance(m, int) and m < 2):
                    dve.wait_ge(branch_steps, m * 2 - 2)
                add_parts(m + T_BRANCH, m4 % 2, 2 * m4, pair=True)

            def branch_body(ub, m0, first):
                for j in range(16):
                    t = j // 4 - 2
                    if j % 4 == 1:
                        if first and t < 0:
                            dve.wait_ge(scaled, HEADS * HEAD_TILES + GATES + t - 1)
                            add_parts(T_BRANCH + t, t % 2, t % 4)
                        else:
                            if first and t == 0:
                                dve.wait_ge(scaled, HEADS * HEAD_TILES + GATES)
                            branch_add(m0 + t, t % 4)
                    split_lo(ub, j)

            branch_body(U_BRANCH, 0, True)
            with dve.Fori(1, 4) as i:
                branch_body(i * 16 + U_BRANCH, i * 4, False)

            def out_body(ub, m0, first):
                for j in range(16):
                    t = j // 4 - 2
                    if first and t < 0:
                        if j % 4 == 1:
                            branch_add(KT + t, t % 4)
                    elif first:
                        if j == 11:
                            dve.wait_ge(branch_steps, 2 * KT)
                        if j in (13, 15):
                            acc_add(2, j // 2 - 6, j // 2 - 6)
                        if j in (11, 13):
                            x_update(2, T_OUT + (j // 2 - 5), j // 2 - 5, j // 2 - 5, j // 2 - 5, False)
                    else:
                        if j % 4 == 1:
                            x_update(2, m0 + (T_OUT + t), m0 + t, t % 2, t % 4, False)
                        if j % 4 == 3:
                            acc_add(2, m0 + t, t % SQ)
                    split_lo(ub, j)

            out_body(U_OUT, 0, True)
            with dve.Fori(1, 4) as i:
                out_body(i * 16 + U_OUT, i * 4, False)

            gu_phase(2, FT, U_GU2, T_GU2)
            down_phase(3, FT, U_DOWN2, T_DOWN2, T_GU2)

            def ple_add(m, s, bank):
                if not (isinstance(m, int) and m < 2):
                    dve.wait_ge(ple_scaled, m - 1)
                add_parts(m + T_PLE, s, bank)

            def ple_y(m, s):
                dve.wait_ge(ple_sig, m + 1)
                nc.vector.tensor_tensor(prod[:, s, :], act2[:, s, :], emb[:, m, :], ALU.mult).then_inc(y_parts, 1)
                dve.wait_ge(y_parts, m * 2 + 1)
                nc.vector.tensor_tensor(y[:, m, :], prod[:, s, :], x[:, m, :], ALU.add).then_inc(y_parts, 1)

            def ple_body(ub, m0, first):
                for j in range(16):
                    t = j // 4 - 2
                    if first:
                        if j == 5:
                            down_update(3, KT - 1, T_DOWN2, True)
                        if j == 7:
                            acc_add(3, KT - 1, (KT - 1) % SQ)
                        if j == 8:
                            proj_add(PROJ_UNITS - 1)
                        if j in (11, 13):
                            ple_add(j // 2 - 5, j // 2 - 5, j // 2 - 5)
                        if j == 15:
                            ple_y(0, 0)
                    else:
                        if j % 4 == 1:
                            ple_add(m0 + t, t % 2, t % 4)
                        if j % 4 == 0:
                            ple_y(m0 + (t - 1), (t - 1) % 2)
                    split_lo(ub, j)

            ple_body(U_PLE, 0, True)
            with dve.Fori(1, 4) as i:
                ple_body(i * 16 + U_PLE, i * 4, False)
            ple_y(13, 1)
            for m in (14, 15):
                ple_add(m, m % 2, m % 4)
                ple_y(m, m % 2)

        @block.gpsimd
        def _(pool):
            def hidden_lo(n, f, p):
                pool.wait_ge(hid_hi, n + 1)
                nc.gpsimd.tensor_tensor(hid[:, f, T:], prod[:, p, :], hid[:, f, 0:T].bitcast(F32),
                                        ALU.subtract).then_inc(hid_lo, 1)

            nc.gpsimd.memset(unread[:], 0.0).then_inc(hid_lo, 2)
            for m in range(KT - ACT_SQ):
                if m % 4 == 0:
                    pool.wait_ge(x_landed[m // 4], 16)
                if m:
                    pool.wait_ge(first_sq, 2 * m)
                square = act2[:, 0, :] if m == 0 else prod[:, 0, :]
                nc.gpsimd.tensor_tensor(square, x[:, m, :], x[:, m, :], ALU.mult).then_inc(first_sq, 1 if m else 2)
                if m:
                    pool.wait_ge(first_sq, 2 * m + 1)
                    nc.gpsimd.tensor_tensor(act2[:, 0, :], act2[:, 0, :], prod[:, 0, :], ALU.add).then_inc(first_sq, 1)
            with pool.Fori(0, FT // 2) as i:
                for p in range(2):
                    hidden_lo(i * 2 + p, i * 2 + p, p)

            pool.wait_ge(unit_used, U_HEADS)
            nc.gpsimd.memset(padded[:], 0.0).then_inc(pad_zero, 1)
            pool.wait_ge(pad_zero, 1)
            pool.wait_ge(const_landed, 16)
            pool.wait_ge(r_ready, 2)

            def scale_tile(n, t, s, out):
                pool.wait_ge(tile_free, n * HEAD_TILES + (T_HEADS + t + 1))
                nc.gpsimd.tensor_tensor(out, whole[:, s, 0:T], r[:], ALU.mult).then_inc(scaled, 1)

            def causal_conv(n, c):
                pool.wait_ge(scaled, n * HEAD_TILES + (c + 1))
                w = lambda i: taps[:, c * CONV_K + i:c * CONV_K + i + 1]
                for i in range(CONV_K):
                    if not (isinstance(n, int) and n == 0 and c == 0 and i == 0):
                        pool.wait_ge(conv_steps, n * (6 * CONV_K) + (2 * (c * CONV_K + i)))
                    nc.gpsimd.tensor_tensor(conv[:, c, :] if i == 0 else tap[:], padded[:, c, i:i + T],
                                            w(i).to_broadcast([P, T]), ALU.mult).then_inc(conv_steps, 1 if i else 2)
                    if i:
                        pool.wait_ge(conv_steps, n * (6 * CONV_K) + (2 * (c * CONV_K + i) + 1))
                        nc.gpsimd.tensor_tensor(conv[:, c, :], conv[:, c, :], tap[:], ALU.add).then_inc(conv_steps, 1)

            def head_period(n, p, kind, tpar):
                g = n - 1
                if kind != "first":
                    scale_tile(g, 5, (tpar - 2) % 2, att[:, 1, :])
                    pool.wait_ge(lmat_ready, g * 2 + 2)
                    nc.gpsimd.tensor_tensor(cmat[:, 0], lmat[:], both(const[:, C_MASKS, :]),
                                            ALU.mult).then_inc(cmat_ready, 1)
                    pool.wait_ge(decay_ready, g * 2 + 2)
                    nc.gpsimd.tensor_tensor(decay[:, 2:4, :], decay[:, 2:4, :], both(upper),
                                            ALU.mult).then_inc(incl_ready, 1)
                    for s in range(1, LEVELS):
                        if s == 2:
                            scale_tile(g, 6, (tpar - 1) % 2, att[:, 2, :])
                        nc.gpsimd.tensor_tensor(cmat[:, s], lmat[:], both(const[:, C_MASKS + s, :]),
                                                ALU.mult).then_inc(cmat_ready, 1)
                if kind != "ghost":
                    if kind != "first":
                        pool.wait_ge(silu_done, n * 2)
                    nc.gpsimd.tensor_copy(taps[:], par[:, bass.ds(n * (3 * CONV_K) + P_CONV, 3 * CONV_K)]
                                          ).then_inc(taps_ready, 1)
                    pool.wait_ge(taps_ready, n + 1)
                    for c in range(3):
                        scale_tile(n, c, (tpar + c) % 2, padded[:, c, CONV_K - 1:])
                        causal_conv(n, c)
                    scale_tile(n, 3, (tpar + 3) % 2, conv[:, 3, :])
                    if kind != "first":
                        pool.wait_ge(att_normed, g * 2 + 2)
                    scale_tile(n, 4, (tpar + 4) % 2, att[:, 0, :])
                else:
                    for t in range(GHOST_GATES - 2):
                        scale_tile(n, t, t % 2, gates[:, t, :])
                if kind != "first":
                    pool.wait_ge(ya_hi, g + 1)
                    nc.gpsimd.tensor_tensor(ya[:, g, T:], y_gdn[:, 1, :], ya[:, g, 0:T].bitcast(F32),
                                            ALU.subtract).then_inc(ya_lo, 1)

            head_period(0, 0, "first", 0)
            with pool.Fori(0, 3) as i:
                head_period(i * 2 + 1, 1, "", 1)
                head_period(i * 2 + 2, 0, "", 0)
            head_period(7, 1, "", 1)
            head_period(8, 0, "ghost", 0)

            pool.wait_ge(yb_lo, HEADS)
            with pool.Fori(0, (GATES - GHOST_GATES + 2) // 2) as i:
                for s in range(2):
                    pool.wait_ge(tile_free, i * 2 + (T_GHOST + GHOST_GATES - 2 + s + 1))
                    nc.gpsimd.tensor_tensor(gates[:, i * 2 + (GHOST_GATES - 2 + s), :], whole[:, s, 0:T], r[:],
                                            ALU.mult).then_inc(scaled, 1)

            def branch_mix(m, s, first):
                pool.wait_ge(sig_ready, m + 1)
                pool.wait_ge(tile_free, m + (T_BRANCH + 1))
                w2 = whole[:, s, :].rearrange("p (a b) -> p a b", a=2)
                nc.gpsimd.tensor_tensor(w2, w2, sig[:, s], ALU.mult).then_inc(branch_steps, 1)
                pool.wait_ge(branch_steps, m * 2 + 1)
                if not first:
                    pool.wait_ge(mixed_lo, m - 1)
                nc.gpsimd.tensor_tensor(mixed_f[:, s, :], whole[:, s, 0:T], whole[:, s, T:],
                                        ALU.add).then_inc(branch_steps, 1)

            def mixed_lo_step(m, s):
                pool.wait_ge(mixed_hi, m + 1)
                nc.gpsimd.tensor_tensor(mixed[:, m, T:], mixed_f[:, s, :], mixed[:, m, 0:T].bitcast(F32),
                                        ALU.subtract).then_inc(mixed_lo, 1)

            branch_mix(0, 0, True)
            branch_mix(1, 1, True)
            mixed_lo_step(0, 0)
            with pool.Fori(1, KT // 2) as i:
                branch_mix(i * 2, 0, False)
                mixed_lo_step(i * 2 - 1, 1)
                branch_mix(i * 2 + 1, 1, False)
                mixed_lo_step(i * 2, 0)
            mixed_lo_step(KT - 1, 1)

            with pool.Fori(FT // 2, FT) as i:
                for p in range(2):
                    hidden_lo(i * 2 + p, i * 2 - FT + p, p)

            with pool.Fori(0, KT // 2) as i:
                pool.wait_ge(r_ready, 4)
                for s in range(2):
                    pool.wait_ge(tile_free, i * 2 + (T_PLE + s + 1))
                    nc.gpsimd.tensor_tensor(gate_s[:, s, :], whole[:, s, 0:T], r[:], ALU.mult).then_inc(ple_scaled, 1)

        @block.tensor
        def _(pe):
            def unit(ub, k, tile_k, n_k, bank, rhs, visit=None):
                pe.wait_ge(lo_ready, ub + (k + 1))
                for i in range(UK):
                    kt = tile_k + i
                    hi, lo = (w[:, k % HL, i * P:(i + 1) * P] for w in (w_hi, w_lo))
                    whole_mm = lambda: nc.tensor.matmul(ps[:, bank, :], hi, rhs(kt),
                                                        start=(kt == 0), stop=(kt == n_k - 1))
                    half_mm = lambda: nc.tensor.matmul(ps[:, bank, 0:T], lo, rhs(kt)[:, 0:T],
                                                       start=False, stop=False)
                    if kt == 0:
                        whole_mm()
                        last = half_mm()
                    else:
                        half_mm()
                        last = whole_mm()
                last.then_inc(unit_used, 1)

            def from_x(kt):
                return xw[:, kt, :]

            def norm_visit(round_):
                pe.wait_ge(ones_set, 1)
                pe.wait_ge(acc_added, KT * (round_ + 1))
                if round_ == 0:
                    pe.wait_ge(first_sq, 2 * (KT - ACT_SQ))
                    nc.tensor.matmul(ps[:, NORM_BANK, 0:T], ones[:], act2[:, 0, :], start=True, stop=False)
                nc.tensor.matmul(ps[:, NORM_BANK, 0:T], ones[:], acc[:], start=(round_ > 0),
                                 stop=True).then_inc(norm_summed, 1)

            def gu_tile(ub, k0, tile, p, first):
                if not first:
                    pe.wait_ge(tile_free, tile - 1)
                for j in range(8):
                    half, q = FIRST_UNITS[j] if first and k0 == 0 else (j // 4, j % 4)
                    if first and k0 == 0 and half == 0:
                        pe.wait_ge(xw_lo, KT * (first - 1) + 4 * q + 4)
                    unit(ub, k0 + j, 4 * q, KT, 2 * p + half, from_x)
                    if first and k0 + j == 10:
                        norm_visit(first - 1)

            def gu_phase(round_, u0, t0):
                if round_:
                    pe.wait_ge(tile_free, t0 - 2)
                gu_tile(u0, 0, t0, 0, round_ + 1)
                if round_:
                    pe.wait_ge(tile_free, t0)
                gu_tile(u0, 8, t0 + 1, 1, round_ + 1)
                with pe.Fori(1, FT // 2) as i:
                    gu_tile(i * 16 + u0, 0, i * 2 + t0, 0, 0)
                    gu_tile(i * 16 + u0, 8, i * 2 + (t0 + 1), 1, 0)

            def proj_unit(b):
                k = down_unit(2 * b + 2, True) - 1
                pe.wait_ge(lo_ready, U_DOWN2 + k + 1)
                for i in range(UK):
                    bank, kt = 4 + 2 * (b % 2) + i // 2, i % 2
                    hi, lo = (w[:, k % HL, i * P:(i + 1) * P] for w in (w_hi, w_lo))
                    if kt == 0:
                        nc.tensor.matmul(ps[:, bank, :], hi, p_hl[:, 0, :], start=True, stop=False)
                        nc.tensor.matmul(ps[:, bank, 0:T], lo, p_hl[:, 0, 0:T], start=False, stop=False)
                    else:
                        nc.tensor.matmul(ps[:, bank, 0:T], lo, p_hl[:, 1, 0:T], start=False, stop=False)
                        last = nc.tensor.matmul(ps[:, bank, :], hi, p_hl[:, 1, :], start=False, stop=True)
                last.then_inc(unit_used, 1)

            def down_phase(n0, u0, t0):
                proj = n0 > 0
                for m in range(KT):
                    pe.wait_ge(tile_free, t0 + (-1 if m == 0 else down_tile(m - 2, proj) if m > 1 else -1))
                    for j in range(FT // UK):
                        if m == 0:
                            if j == 0:
                                pe.wait_ge(hid_lo, n0 + FT)
                            if j == 10:
                                pe.wait_ge(hid_lo, n0 + FT + 2)
                        unit(u0, down_unit(m, proj) + j, 4 * j, FT, m % 4, lambda kt: hid[:, kt, :])
                    if proj and m % 2:
                        if m == 1:
                            pe.wait_ge(p_lo, 1)
                        proj_unit(m // 2)

            gu_phase(0, U_GU1, T_GU1)
            down_phase(0, U_DOWN1, T_DOWN1)

            def head_period(ub, k0, n, p, kind):
                g, q = n - 1, 1 - p
                tile0 = T_HEADS + HEAD_TILES * n
                ghost = kind == "ghost"
                for j in range(32 if ghost else HEAD_UNITS):
                    t, k = FIRST_UNITS[j] if kind == "first" and j < 8 else (j // 4, j % 4)
                    if k == 0:
                        pe.wait_ge(tile_free, tile0 + (t - 2))
                    if kind == "first" and t == 0:
                        pe.wait_ge(xw_lo, KT + 4 * k + 4)
                    unit(ub, k0 + j, 4 * k, KT, t % 4 if ghost else BANK_OF_HEAD_TILE[t], from_x)
                    if kind == "first":
                        if j == 7:
                            norm_visit(1)
                            pe.wait_ge(wab_lo_ready, 1)
                            for kt in range(KT):
                                w_h, w_l = (w[:, kt * 2 * HEADS:(kt + 1) * 2 * HEADS] for w in (wab_hi, wab_lo))
                                if kt == 0:
                                    nc.tensor.matmul(ps[0:2 * HEADS, 5, :], w_h, xw[:, kt, :], start=True, stop=False)
                                nc.tensor.matmul(ps[0:2 * HEADS, 5, 0:T], w_l, xw[:, kt, 0:T], start=False, stop=False)
                                if kt > 0:
                                    last = nc.tensor.matmul(ps[0:2 * HEADS, 5, :], w_h, xw[:, kt, :], start=False,
                                                            stop=(kt == KT - 1))
                            last.then_inc(ab_product, 1)
                        if j == 8:
                            pe.wait_ge(const_landed, 16)
                            pe.wait_ge(ab_steps, 2)
                            for c in range(2):
                                last = nc.tensor.transpose(ps[:, 6, c * 2 * HEADS:(c + 1) * 2 * HEADS],
                                                           ab_row[:, 1, c * GC:(c + 1) * GC],
                                                           const[0:2 * HEADS, C_IDENT, 0:2 * HEADS])
                            last.then_inc(ab_ready, 1)
                        if j == 15:
                            pe.wait_ge(ab_steps, 9)
                            g_all = cols[:, K_G:K_G + 2, :].rearrange("p a b -> p (a b)")
                            nc.tensor.matmul(ps[:, 5, 64:80], upper, g_all, start=True, stop=True)
                            nc.tensor.matmul(ps[:, 5, 80:96], ones[:], g_all, start=True, stop=True).then_inc(gc_summed, 1)
                    else:
                        if j == 0:
                            pe.wait_ge(upper_ready, g * 2 + 2)
                            nc.tensor.matmul(ps[:, 5, 0:T], ones[:], upper_g[:].rearrange("p a b -> p (a b)"),
                                             start=True, stop=True)
                            pe.wait_ge(qk_normed, g * 2 + 2)
                            nc.tensor.transpose(ps[:, 5, 2 * GC:3 * GC], kn[:, 0:GC], ident).then_inc(gc_ready, 1)
                            for c in range(2):
                                k_c = kn[:, c * GC:(c + 1) * GC]
                                nc.tensor.matmul(ps[:, 4, c * GC:(c + 1) * GC], k_c, k_c, start=True, stop=True)
                                last = nc.tensor.matmul(ps[:, 4, (2 + c) * GC:(3 + c) * GC], k_c,
                                                        qn[:, c * GC:(c + 1) * GC], start=True, stop=True)
                            last.then_inc(gram_ready, 1)
                        if j == 2:
                            pe.wait_ge(cmat_ready, g * LEVELS + 1)
                            pe.wait_ge(v_copied, g + 1)
                            for c in range(2):
                                last = nc.tensor.transpose(ps[:, 6, c * GC:(c + 1) * GC], cmat[:, 0, c, :], ident)
                            last.then_inc(c0_turned, 1)
                        if j >= 3 and j % 2 == 1 and j <= 13:
                            s = (j - 1) // 2
                            if s == 1:
                                pe.wait_ge(k_tail_ready, g + 1)
                            pe.wait_ge(cmat_ready, g * LEVELS + (s + 1))
                            pe.wait_ge(inv_ready, g * LEVELS + s)
                            for c in range(2):
                                last = nc.tensor.matmul(ps[:, 5, c * GC:(c + 1) * GC], cmat[:, s, c, :],
                                                        inv[:, 2 + c, :], start=True, stop=True)
                            last.then_inc(t1_ready, 1)
                        if j >= 4 and j % 2 == 0 and j <= 14:
                            s = (j - 2) // 2
                            pe.wait_ge(t1_copied, g * 6 + s)
                            if s == 1:
                                pe.wait_ge(a_qk_ready, g + 1)
                            for c in range(2):
                                if s < 6:
                                    nc.tensor.matmul(ps[:, 4, c * GC:(c + 1) * GC], t1[:, c, :], inv[:, c, :],
                                                     start=True, stop=True)
                                last = nc.tensor.matmul(ps[:, 4, (2 + c) * GC:(3 + c) * GC], inv[:, c, :],
                                                        t1[:, c, :], start=True, stop=True)
                            last.then_inc(step_ready, 1)
                        if j == 15:
                            pe.wait_ge(inv_ready, g * LEVELS + LEVELS)
                            pe.wait_ge(rhs0_ready, g + 1)
                            nc.tensor.matmul(ps[:, 6, 0:DH], inv[:, 2, :], rhs0[:], start=True,
                                             stop=True).then_inc(v0_ready, 1)
                        if j == 16:
                            pe.wait_ge(v0_copied, g + 1)
                            nc.tensor.matmul(ps[:, 6, DH:2 * DH], k_tail[:], v_new[:, 0, :], start=True,
                                             stop=True).then_inc(state_ready, 1)
                            nc.tensor.matmul(ps[:, 4, 0:GC], v_new[:, 0, :], a_qk[:, 0, :], start=True, stop=True)
                        if j == 17:
                            pe.wait_ge(state_copied, g + 1)
                            nc.tensor.matmul(ps[:, 6, 2 * DH:3 * DH], kn[:, GC:], state[:], start=True,
                                             stop=True).then_inc(ks_ready, 1)
                        if j == 18:
                            pe.wait_ge(rhs1_steps, g * 2 + 2)
                            nc.tensor.matmul(ps[:, 6, 3 * DH:4 * DH], inv[:, 3, :], rhs1[:, 1, :], start=True,
                                             stop=True).then_inc(v1_ready, 1)
                        if j == 19:
                            pe.wait_ge(v1_copied, g + 1)
                            pe.wait_ge(qe_ready, g + 1)
                            nc.tensor.matmul(ps[:, 4, GC:2 * GC], state[:], qe[:], start=True, stop=False)
                            nc.tensor.matmul(ps[:, 4, GC:2 * GC], v_new[:, 1, :], a_qk[:, 1, :], start=False,
                                             stop=True).then_inc(o_ready, 1)
                        if j == 20:
                            pe.wait_ge(o_sq_ready, g + 1)
                            nc.tensor.matmul(ps[:, 5, 0:T], ones[:], o_sq[:], start=True, stop=True).then_inc(o_summed, 1)
                        if j == 5:
                            pe.wait_ge(scaled, g * HEAD_TILES + 7)
                            for c in range(2):
                                last = nc.tensor.transpose(ps[:, 7, c * GC:(c + 1) * GC],
                                                           att[:, 2, c * GC:(c + 1) * GC], ident)
                            last.then_inc(av_turned, 1)
                        if j == 6:
                            pe.wait_ge(att_sq_ready, g + 1)
                            pe.wait_ge(av_copied, g + 1)
                            nc.tensor.matmul(ps[:, 7, :], ones[:], att_sq[:].rearrange("p a b -> p (a b)"),
                                             start=True, stop=True).then_inc(att_summed, 1)
                        if j == 9:
                            pe.wait_ge(att_normed, g * 2 + 2)
                            nc.tensor.matmul(ps[:, 7, 0:GC], att_n[:, 0, 0:GC], att_n[:, 1, 0:GC], start=True, stop=True)
                            nc.tensor.matmul(ps[:, 7, GC:SCORES], att_n[:, 0, GC:], att_n[:, 1, :], start=True,
                                             stop=True).then_inc(score_ready, 1)
                        if j == 12:
                            pe.wait_ge(prob_ready, g * 2 + 2)
                            for c in range(3):
                                last = nc.tensor.transpose(ps[:, 7, c * GC:(c + 1) * GC], score[:, c * GC:(c + 1) * GC],
                                                           ident)
                            last.then_inc(prob_turned, 1)
                        if j == 13:
                            pe.wait_ge(prob_copied, g + 1)
                            nc.tensor.matmul(ps[:, 7, 0:T], av_tok[:, 0, :], prob_t[:, 0:T], start=True, stop=False)
                            nc.tensor.matmul(ps[:, 7, GC:T], av_tok[:, 1, :], prob_t[:, T:], start=False,
                                             stop=True).then_inc(att_o_ready, 1)
                    if j == 22 and not ghost:
                        pe.wait_ge(qk_sq_ready, n + 1)
                        if kind != "first":
                            pe.wait_ge(yb_lo, n)
                        nc.tensor.matmul(ps[:, 7, :], ones[:], qk_sq[:].rearrange("p a b -> p (a b)"), start=True,
                                         stop=True).then_inc(qk_summed, 1)
                        for c in range(2):
                            last = nc.tensor.transpose(ps[:, 6, c * GC:(c + 1) * GC],
                                                       qkvz[:, p, 2, c * GC:(c + 1) * GC], ident)
                        last.then_inc(v_turned, 1)

            head_period(U_HEADS, 0, 0, 0, "first")
            with pe.Fori(0, 3) as i:
                head_period(i * 56 + U_HEADS, 28, i * 2 + 1, 1, "")
                head_period(i * 56 + U_HEADS, 56, i * 2 + 2, 0, "")
            head_period(U_HEADS + 168, 28, 7, 1, "")
            head_period(U_GHOST, 0, 8, 0, "ghost")

            with pe.Fori(0, (GATES - GHOST_GATES) // 4) as i:
                for j in range(16):
                    if j % 4 == 0:
                        pe.wait_ge(tile_free, i * 4 + (T_GHOST + GHOST_GATES + j // 4 - 2))
                    unit(i * 16 + U_GATES, j, 4 * (j % 4), KT, j // 4, from_x)

            def branch_body(ub, m0, first):
                for t in range(4):
                    pe.wait_ge(tile_free, m0 + (T_BRANCH + t - (1 if first and t == 1 else 2)))
                    for j in range(4):
                        src = ya if j < 2 else yb
                        unit(ub, 4 * t + j, 4 * (j % 2), HEADS, 2 * t + j // 2, lambda kt, src=src: src[:, kt, :])

            pe.wait_ge(ya_lo, HEADS)
            pe.wait_ge(yb_lo, HEADS)
            branch_body(U_BRANCH, 0, True)
            with pe.Fori(1, 4) as i:
                branch_body(i * 16 + U_BRANCH, i * 4, False)

            def out_body(ub, m0, first):
                for j in range(16):
                    t, k = FIRST_UNITS[j] if first and j < 8 else (j // 4, j % 4)
                    if k == 0:
                        pe.wait_ge(tile_free, m0 + (T_OUT + (-2 if first and t == 1 else t - 2)))
                    if first and t == 0:
                        pe.wait_ge(mixed_lo, 4 * k + 4)
                    unit(ub, j, 4 * k, KT, t, lambda kt: mixed[:, kt, :])

            out_body(U_OUT, 0, True)
            with pe.Fori(1, 4) as i:
                out_body(i * 16 + U_OUT, i * 4, False)

            gu_phase(2, U_GU2, T_GU2)
            down_phase(FT, U_DOWN2, T_DOWN2)

            def ple_body(ub, m0, first):
                for j in range(16):
                    t, k = FIRST_UNITS[j] if first and j < 8 else (j // 4, j % 4)
                    if k == 0:
                        pe.wait_ge(tile_free, m0 + (T_PLE + (-3 if first and t < 2 else t - 2)))
                    if first and t == 0:
                        pe.wait_ge(xw_lo, 3 * KT + 4 * k + 4)
                    unit(ub, j, 4 * k, KT, t, from_x)
                    if first and j == 7:
                        pe.wait_ge(tile_free, T_PLE)
                        norm_visit(3)

            ple_body(U_PLE, 0, True)
            with pe.Fori(1, 4) as i:
                ple_body(i * 16 + U_PLE, i * 4, False)


def weight_units(w):
    k, m = w.shape
    return w.reshape(k // UC, UK, P, m // P, P).transpose(3, 0, 2, 1, 4).reshape(m // P, k // UC, P, UC)


def first_tiles(units):
    order = [4 * t + k for t, k in FIRST_UNITS]
    return np.concatenate([units[order], units[len(order):]])


def pack_weights(i):
    ffn = []
    for name in ("ffn1", "ffn2"):
        gu = i[f"{name}_w_gu"][0]
        gate, up = weight_units(gu[:, :FF]), weight_units(gu[:, FF:])
        ffn.append([first_tiles(np.concatenate([gate, up], 1).reshape(-1, P, UC)),
                    weight_units(i[f"{name}_w_down"][0]).reshape(-1, P, UC)])
    w_in, width = i["w_in"][0], HEADS * DH
    z = 3 * width
    att = z + width + 2 * HEADS
    gate = att + 3 * width
    tiles = [weight_units(w_in[:, o:o + width]) for o in
             (0, width, 2 * width, z, att, att + width, att + 2 * width)]
    heads = first_tiles(np.stack(tiles, 1).reshape(-1, P, UC))
    gates = np.stack([weight_units(w_in[:, gate:gate + D]), weight_units(w_in[:, gate + D:])], 1).reshape(-1, P, UC)
    branch = np.concatenate([weight_units(i["w_branch_a"][0]), weight_units(i["w_branch_b"][0])], 1).reshape(-1, P, UC)
    proj = i["ple_proj"][0].reshape(2, P, KT // 2, 2, P).transpose(2, 1, 3, 0, 4).reshape(-1, P, UC)
    down = ffn[1][1].reshape(PROJ_UNITS, -1, P, UC)
    ffn[1][1] = np.concatenate([down, proj[:, None]], 1).reshape(-1, P, UC)
    units = np.concatenate([*ffn[0], heads, gates, branch,
                            first_tiles(weight_units(i["w_out"][0]).reshape(-1, P, UC)), *ffn[1],
                            first_tiles(weight_units(i["ple_gate"][0]).reshape(-1, P, UC))])
    assert len(units) == UNITS
    return units.reshape(UNITS // 2, 2, P, UC).transpose(0, 2, 1, 3).reshape(UNITS // 2, P, 2 * UC)


def constants():
    a = np.arange(P)
    row, colm = a[:, None], a[None, :]
    parts = [np.eye(P), row <= colm]
    for s in range(LEVELS):
        parts.append((row >> (s + 1) == colm >> (s + 1)) & ((row >> s) & 1 == 1) & ((colm >> s) & 1 == 0))
    return np.stack(parts, 1).astype(np.float32)


def kernel(**inputs):
    import concourse.bacc as bacc
    from concourse.bass_utils import run_bass_kernel_spmd

    i = {k: np.asarray(v) for k, v in inputs.items()}

    def blocks(v):
        return np.swapaxes(v.reshape(-1, P, *v.shape[1:]), 0, 1)

    def rows(v):
        return np.broadcast_to(v, (P, v.size))

    conv = i["conv_w"][0].reshape(CONV_K, 3, HEADS, P).transpose(3, 2, 1, 0).reshape(P, -1)
    params = np.concatenate(
        [blocks(i[n][0]) for n in ("ffn1_norm", "mix_norm", "ffn2_norm", "ple_norm")] + [conv]
        + [i[n][0].reshape(P, 1) for n in ("gdn_norm", "q_norm", "k_norm")]
        + [rows(i["dt_bias"][0]), rows(i["a_log"][0])], 1)
    assert params.shape == (P, N_PARAM)
    w_in = i["w_in"][0]
    ab0 = 4 * HEADS * DH
    query = np.concatenate([np.tile(np.arange(P)[:, None], (1, GC)), np.tile(P + np.arange(P)[:, None], (1, T))], 1)
    key = np.concatenate([np.arange(GC), np.arange(T)])[None, :]
    rel = np.clip(query - key, -(CHUNK - 1), MAX_REL) + (CHUNK - 1)
    bias = np.where(key // CHUNK <= query // CHUNK, i["rel_bias"][0][:, rel], np.float32(NEG_INF))
    arrays = {
        "wstream": pack_weights(i),
        "x_t": blocks(i["x"][0].T),
        "p_t": blocks(i["p"][0, 0].T),
        "consts": constants(),
        "params": params,
        "w_ab": blocks(w_in[:, ab0:ab0 + 2 * HEADS]).reshape(P, -1),
        "rel_bias_rows": bias.transpose(1, 0, 2),
    }
    arrays = {k: np.ascontiguousarray(v) for k, v in arrays.items()}
    nc = bacc.Bacc("TRN2", target_bir_lowering=False, num_devices=1, dynamic_dma_scratch_size=1024)
    args = [nc.dram_tensor(k, v.shape, F32, kind="ExternalInput").ap() for k, v in arrays.items()]
    out = nc.dram_tensor("y_t", (4, P, 4, T), F32, kind="ExternalOutput").ap()
    build(nc, *args, out)
    got = run_bass_kernel_spmd(nc, [arrays], core_ids=[0]).results[0]["y_t"]
    return np.ascontiguousarray(got.transpose(0, 2, 1, 3).reshape(D, T).T)[None]
```
